# Optimizing a Trainium2 kernel written in Bass

```python
import jax, jax.numpy as jnp
from jax import lax
import numpy as np
import math

D_MODEL = 1024
BATCH = 1
SEQ = 256
DEPTH = 2

GRID_W = 64
CTX_LEN = 256
N_MIXERS = 2
HEAD_DIM = 64
NORM_EPS = 1e-6
ATTN_SCALE = HEAD_DIM ** -0.5
A_HEADS = 16
A_KV_HEADS = 4
A_GROUP = A_HEADS // A_KV_HEADS
A_WIDTH = A_HEADS * HEAD_DIM
A_KV_WIDTH = A_KV_HEADS * HEAD_DIM
A_IN = 2 * A_WIDTH + 2 * A_KV_WIDTH
ROPE_THETA = 10000.0
ROPE_AXIS_DIM = HEAD_DIM // 2
ROPE_HALF = ROPE_AXIS_DIM // 2
Q_BLOCK = 128
B_HEADS = 16
B_WIDTH = B_HEADS * HEAD_DIM
B_IN = 4 * B_WIDTH
WIN_R = 8
WIN_C = 16
N_A_LAYERS = (DEPTH + N_MIXERS - 1) // N_MIXERS
N_B_LAYERS = DEPTH // N_MIXERS


def rms_norm(x, g):
    xf = x.astype(jnp.float32)
    y = xf * lax.rsqrt(jnp.mean(xf * xf, axis=-1, keepdims=True) + NORM_EPS)
    return (y * g.astype(jnp.float32)).astype(x.dtype)

def axial_rope_tables(t_len):
    pos = jnp.arange(t_len, dtype=jnp.int32)
    row = (pos // GRID_W).astype(jnp.float32)
    col = (pos % GRID_W).astype(jnp.float32)
    inv = ROPE_THETA ** (-jnp.arange(0, ROPE_AXIS_DIM, 2, dtype=jnp.float32) / ROPE_AXIS_DIM)
    ang = jnp.stack([row[:, None] * inv, col[:, None] * inv], axis=1)
    return jnp.cos(ang), jnp.sin(ang)

def apply_axial_rope(x, cos, sin):
    shp = x.shape
    xs = x.reshape(shp[0], shp[1], shp[2], 2, 2, ROPE_HALF)
    x1 = xs[..., 0, :]
    x2 = xs[..., 1, :]
    cc = cos.astype(x.dtype)[None, :, None]
    ss = sin.astype(x.dtype)[None, :, None]
    out = jnp.stack([x1 * cc - x2 * ss, x2 * cc + x1 * ss], axis=-2)
    return out.reshape(shp)

def gqa_axial_mixer(hx, hc, w_in, q_g, k_g, w_out, cos, sin, need_ctx_out):
    b, t, _ = hx.shape
    lc = hc.shape[1]
    px = hx @ w_in
    q = px[..., :A_WIDTH].reshape(b, t, A_HEADS, HEAD_DIM)
    k = px[..., A_WIDTH:A_WIDTH + A_KV_WIDTH].reshape(b, t, A_KV_HEADS, HEAD_DIM)
    v = px[..., A_WIDTH + A_KV_WIDTH:A_WIDTH + 2 * A_KV_WIDTH].reshape(b, t, A_KV_HEADS, HEAD_DIM)
    z = px[..., A_WIDTH + 2 * A_KV_WIDTH:]
    q = apply_axial_rope(rms_norm(q, q_g), cos, sin)
    k = apply_axial_rope(rms_norm(k, k_g), cos, sin)
    pkv = hc @ w_in[:, A_WIDTH:A_WIDTH + 2 * A_KV_WIDTH]
    kc = rms_norm(pkv[..., :A_KV_WIDTH].reshape(b, lc, A_KV_HEADS, HEAD_DIM), k_g)
    vc = pkv[..., A_KV_WIDTH:].reshape(b, lc, A_KV_HEADS, HEAD_DIM)
    k_all = jnp.concatenate([kc, k], axis=1)
    v_all = jnp.concatenate([vc, v], axis=1)
    n_blk = t // Q_BLOCK
    qb = q.reshape(b, n_blk, Q_BLOCK, A_KV_HEADS, A_GROUP, HEAD_DIM).transpose(1, 0, 2, 3, 4, 5)

    def block(qi):
        s = jnp.einsum('bqkgd,bskd->bkgqs', qi, k_all).astype(jnp.float32) * ATTN_SCALE
        p = jax.nn.softmax(s, axis=-1).astype(v_all.dtype)
        return jnp.einsum('bkgqs,bskd->bqkgd', p, v_all)

    o = lax.map(block, qb)
    o = o.transpose(1, 0, 2, 3, 4, 5).reshape(b, t, A_WIDTH)
    yx = (o * jax.nn.silu(z)) @ w_out
    if not need_ctx_out:
        return yx, None
    qc = rms_norm((hc @ w_in[:, :A_WIDTH]).reshape(b, lc, A_HEADS, HEAD_DIM), q_g)
    qc = qc.reshape(b, lc, A_KV_HEADS, A_GROUP, HEAD_DIM)
    zc = hc @ w_in[:, A_WIDTH + 2 * A_KV_WIDTH:]
    sc = jnp.einsum('bqkgd,bskd->bkgqs', qc, kc).astype(jnp.float32) * ATTN_SCALE
    pc = jax.nn.softmax(sc, axis=-1).astype(vc.dtype)
    oc = jnp.einsum('bkgqs,bskd->bqkgd', pc, vc).reshape(b, lc, A_WIDTH)
    yc = (oc * jax.nn.silu(zc)) @ w_out
    return yx, yc

def neighbourhood_mixer(hx, hc, w_in, rpb, w_out, need_ctx_out):
    b, t, _ = hx.shape
    lc = hc.shape[1]
    rows = t // GRID_W
    wr = min(WIN_R, rows)
    px = hx @ w_in
    q = px[..., :B_WIDTH].reshape(b, rows, GRID_W, B_HEADS, HEAD_DIM)
    k = px[..., B_WIDTH:2 * B_WIDTH].reshape(b, rows, GRID_W, B_HEADS, HEAD_DIM)
    v = px[..., 2 * B_WIDTH:3 * B_WIDTH].reshape(b, rows, GRID_W, B_HEADS, HEAD_DIM)
    z = px[..., 3 * B_WIDTH:]
    pkv = hc @ w_in[:, B_WIDTH:3 * B_WIDTH]
    kc = pkv[..., :B_WIDTH].reshape(b, lc, B_HEADS, HEAD_DIM)
    vc = pkv[..., B_WIDTH:].reshape(b, lc, B_HEADS, HEAD_DIM)
    qcol = np.arange(GRID_W)
    c0 = np.clip(qcol - WIN_C // 2, 0, GRID_W - WIN_C)
    col_idx = c0[:, None] + np.arange(WIN_C)[None, :]
    dc_idx = col_idx - qcol[:, None] + (WIN_C - 1)
    n_nb = wr * WIN_C

    def row_block(r):
        r0 = jnp.clip(r - wr // 2, 0, rows - wr)
        kb = lax.dynamic_slice_in_dim(k, r0, wr, axis=1)
        vb = lax.dynamic_slice_in_dim(v, r0, wr, axis=1)
        kw = kb[:, :, col_idx].transpose(0, 2, 1, 3, 4, 5).reshape(b, GRID_W, n_nb, B_HEADS, HEAD_DIM)
        vw = vb[:, :, col_idx].transpose(0, 2, 1, 3, 4, 5).reshape(b, GRID_W, n_nb, B_HEADS, HEAD_DIM)
        qr = lax.dynamic_index_in_dim(q, r, axis=1, keepdims=False)
        dr_idx = r0 + jnp.arange(wr) - r + (WIN_R - 1)
        bias = rpb[:, dr_idx][:, :, dc_idx]
        bias = bias.transpose(0, 2, 1, 3).reshape(B_HEADS, GRID_W, n_nb).astype(jnp.float32)
        s_nb = jnp.einsum('bqhd,bqkhd->bhqk', qr, kw).astype(jnp.float32) * ATTN_SCALE + bias
        s_cx = jnp.einsum('bqhd,bshd->bhqs', qr, kc).astype(jnp.float32) * ATTN_SCALE
        p = jax.nn.softmax(jnp.concatenate([s_nb, s_cx], axis=-1), axis=-1).astype(vw.dtype)
        return (jnp.einsum('bhqk,bqkhd->bqhd', p[..., :n_nb], vw)
                + jnp.einsum('bhqs,bshd->bqhd', p[..., n_nb:], vc))

    o = lax.map(row_block, jnp.arange(rows))
    o = o.transpose(1, 0, 2, 3, 4).reshape(b, t, B_WIDTH)
    yx = (o * jax.nn.silu(z)) @ w_out
    if not need_ctx_out:
        return yx, None
    qc = (hc @ w_in[:, :B_WIDTH]).reshape(b, lc, B_HEADS, HEAD_DIM)
    zc = hc @ w_in[:, 3 * B_WIDTH:]
    sc = jnp.einsum('bqhd,bshd->bhqs', qc, kc).astype(jnp.float32) * ATTN_SCALE
    pc = jax.nn.softmax(sc, axis=-1).astype(vc.dtype)
    oc = jnp.einsum('bhqs,bshd->bqhd', pc, vc).reshape(b, lc, B_WIDTH)
    yc = (oc * jax.nn.silu(zc)) @ w_out
    return yx, yc

def first_inputs(seed: int = 0) -> dict:
    key = jax.random.key(seed)
    ks = jax.random.split(key, 20)
    f32 = jnp.float32
    d = D_MODEL
    nrm = lambda k, shp, s: (jax.random.normal(k, shp, f32) * s)
    return {
        "x": nrm(ks[0], (BATCH, SEQ, d), 1.0),
        "c": nrm(ks[1], (BATCH, d), 1.0),
        "ctx": nrm(ks[2], (BATCH, CTX_LEN, d), 1.0),
        "c_ctx": nrm(ks[3], (d,), 1.0),
        "norm_g": 1.0 + nrm(ks[4], (DEPTH, d), 0.02),
        "w_mod": nrm(ks[5], (DEPTH, d, 3 * d), 0.5 * d ** -0.5),
        "b_mod": nrm(ks[6], (DEPTH, 3 * d), 0.01),
        "a_w_in": nrm(ks[7], (N_A_LAYERS, d, A_IN), d ** -0.5),
        "a_q_norm_g": 1.0 + nrm(ks[8], (N_A_LAYERS, HEAD_DIM), 0.02),
        "a_k_norm_g": 1.0 + nrm(ks[9], (N_A_LAYERS, HEAD_DIM), 0.02),
        "a_w_out": nrm(ks[10], (N_A_LAYERS, A_WIDTH, d), A_WIDTH ** -0.5),
        "b_w_in": nrm(ks[11], (N_B_LAYERS, d, B_IN), d ** -0.5),
        "b_rpb": nrm(ks[12], (N_B_LAYERS, B_HEADS, 2 * WIN_R - 1, 2 * WIN_C - 1), 0.02),
        "b_w_out": nrm(ks[13], (N_B_LAYERS, B_WIDTH, d), B_WIDTH ** -0.5),
        "final_norm_g": 1.0 + nrm(ks[14], (d,), 0.02),
    }

def first_block(x, c, ctx, c_ctx, norm_g, w_mod, b_mod, a_w_in, a_q_norm_g, a_k_norm_g, a_w_out,
              b_w_in, b_rpb, b_w_out, final_norm_g):
    t = x.shape[1]
    cos, sin = axial_rope_tables(t)
    silu_c = jax.nn.silu(c)
    silu_cc = jax.nn.silu(c_ctx)
    ia = 0
    ib = 0
    for i in range(DEPTH):
        last = i == DEPTH - 1
        mod_x = (silu_c @ w_mod[i] + b_mod[i])[:, None, :]
        mod_c = silu_cc @ w_mod[i] + b_mod[i]
        sh_x, sc_x, g_x = jnp.split(mod_x, 3, axis=-1)
        sh_c, sc_c, g_c = jnp.split(mod_c, 3, axis=-1)
        hx = rms_norm(x, norm_g[i]) * (1.0 + sc_x) + sh_x
        hc = rms_norm(ctx, norm_g[i]) * (1.0 + sc_c) + sh_c
        if i % N_MIXERS == 0:
            yx, yc = gqa_axial_mixer(hx, hc, a_w_in[ia], a_q_norm_g[ia], a_k_norm_g[ia], a_w_out[ia],
                                     cos, sin, not last)
            ia += 1
        else:
            yx, yc = neighbourhood_mixer(hx, hc, b_w_in[ib], b_rpb[ib], b_w_out[ib], not last)
            ib += 1
        x = x + g_x * yx
        if not last:
            ctx = ctx + g_c * yc
    return rms_norm(x, final_norm_g)


N_HEADS = 16
HEAD_DIM_2 = D_MODEL // N_HEADS
MOBA_BLOCK = 256
MOBA_TOPK = 3
N_BUCKETS = 32
MAX_DISTANCE = 128
D_FF = 2816
N_EXPERTS = 8
TOP_K = 2
D_FF_EXPERT = 3584
N_DENSE = (DEPTH + 1) // 2
N_MOE = DEPTH // 2
RMS_EPS = 1e-6
NEG_BIG = -1e30


def rmsnorm(x, g):
    xf = x.astype(jnp.float32)
    y = xf * lax.rsqrt(jnp.mean(xf * xf, axis=-1, keepdims=True) + RMS_EPS)
    return (y * g.astype(jnp.float32)).astype(x.dtype)

def t5_bucket(dist):
    n = jnp.maximum(dist, 0)
    max_exact = N_BUCKETS // 2
    nf = jnp.maximum(n, 1).astype(jnp.float32)
    large = max_exact + (jnp.log(nf / max_exact) / math.log(MAX_DISTANCE / max_exact)
                         * (N_BUCKETS - max_exact)).astype(jnp.int32)
    large = jnp.minimum(large, N_BUCKETS - 1)
    return jnp.where(n < max_exact, n, large)

def qkv_heads(h, w_qkv):
    b, s, d = h.shape
    qkv = jnp.einsum('bsd,de->bse', h, w_qkv)
    q, k, v = jnp.split(qkv, 3, axis=-1)
    to_heads = lambda t: t.reshape(b, s, N_HEADS, HEAD_DIM_2).transpose(0, 2, 1, 3)
    return to_heads(q), to_heads(k), to_heads(v)

def stick_breaking_attention(q, k, v):
    b, nh, s, dh = q.shape
    scale = dh ** -0.5
    k_pos = jnp.arange(s)

    def block(c):
        q0 = c * Q_BLOCK
        qc = lax.dynamic_slice_in_dim(q, q0, Q_BLOCK, axis=2)
        z = jnp.einsum('bhqd,bhkd->bhqk', qc, k).astype(jnp.float32) * scale
        q_pos = q0 + jnp.arange(Q_BLOCK)
        past = k_pos[None, :] < q_pos[:, None]
        log_one_minus = jnp.where(past, jax.nn.log_sigmoid(-z), 0.0)
        after = lax.cumsum(log_one_minus, axis=3, reverse=True) - log_one_minus
        w = jnp.where(past, jnp.exp(jax.nn.log_sigmoid(z) + after), 0.0)
        return jnp.einsum('bhqk,bhkd->bhqd', w.astype(v.dtype), v)

    out = lax.map(block, jnp.arange(s // Q_BLOCK))
    return out.transpose(1, 2, 0, 3, 4).reshape(b, nh, s, dh)

def moba_attention(q, k, v, rel_bias):
    b, nh, s, dh = q.shape
    scale = dh ** -0.5
    n_blk = -(-s // MOBA_BLOCK)
    s_pad = n_blk * MOBA_BLOCK
    pad = ((0, 0), (0, 0), (0, s_pad - s), (0, 0))
    kb = jnp.pad(k, pad).reshape(b, nh, n_blk, MOBA_BLOCK, dh)
    vb = jnp.pad(v, pad).reshape(b, nh, n_blk, MOBA_BLOCK, dh)
    k_mean = jnp.mean(kb, axis=3)
    n_sel = min(MOBA_TOPK, n_blk - 1)
    bias_hb = rel_bias.T
    in_blk = jnp.arange(MOBA_BLOCK)
    bi = jnp.arange(b)[:, None, None, None]
    hi = jnp.arange(nh)[None, :, None, None]

    def block(c):
        q0 = c * Q_BLOCK
        own = q0 // MOBA_BLOCK
        qc = lax.dynamic_slice_in_dim(q, q0, Q_BLOCK, axis=2)
        q_pos = q0 + jnp.arange(Q_BLOCK)
        k_own = lax.dynamic_index_in_dim(kb, own, axis=2, keepdims=False)
        v_own = lax.dynamic_index_in_dim(vb, own, axis=2, keepdims=False)
        dist_own = q_pos[:, None] - (own * MOBA_BLOCK + in_blk)[None, :]
        logit_own = (jnp.einsum('bhqd,bhkd->bhqk', qc, k_own).astype(jnp.float32) * scale
                     + bias_hb[:, t5_bucket(dist_own)])
        logit_own = jnp.where(dist_own >= 0, logit_own, NEG_BIG)
        if n_sel == 0:
            p_own = jax.nn.softmax(logit_own, axis=-1).astype(v.dtype)
            return jnp.einsum('bhqk,bhkd->bhqd', p_own, v_own)
        gate = jnp.einsum('bhqd,bhnd->bhqn', qc, k_mean).astype(jnp.float32)
        gate = jnp.where(jnp.arange(n_blk) < own, gate, NEG_BIG)
        _, idx = lax.top_k(gate, n_sel)
        valid = idx < own
        k_sel = kb[bi, hi, idx]
        v_sel = vb[bi, hi, idx]
        dist_sel = q_pos[:, None, None] - (idx[..., None] * MOBA_BLOCK + in_blk)
        logit_sel = (jnp.einsum('bhqd,bhqnkd->bhqnk', qc, k_sel).astype(jnp.float32) * scale
                     + bias_hb[hi[..., None], t5_bucket(dist_sel)])
        logit_sel = jnp.where(valid[..., None], logit_sel, NEG_BIG)
        n_s = n_sel * MOBA_BLOCK
        logits = jnp.concatenate([logit_sel.reshape(b, nh, Q_BLOCK, n_s), logit_own], axis=-1)
        p = jax.nn.softmax(logits, axis=-1).astype(v.dtype)
        p_sel = p[..., :n_s].reshape(b, nh, Q_BLOCK, n_sel, MOBA_BLOCK)
        p_own = p[..., n_s:]
        return (jnp.einsum('bhqnk,bhqnkd->bhqd', p_sel, v_sel)
                + jnp.einsum('bhqk,bhkd->bhqd', p_own, v_own))

    out = lax.map(block, jnp.arange(s // Q_BLOCK))
    return out.transpose(1, 2, 0, 3, 4).reshape(b, nh, s, dh)

def swiglu(h, w1, w3, w2):
    hid = jax.nn.silu(jnp.einsum('bsd,df->bsf', h, w1)) * jnp.einsum('bsd,df->bsf', h, w3)
    return jnp.einsum('bsf,fd->bsd', hid, w2)

def moe_swiglu(h, w_router, w1, w3, w2):
    b, s, d = h.shape
    t = h.reshape(b * s, d)
    logits = jnp.dot(t, w_router).astype(jnp.float32)
    top_val, top_idx = lax.top_k(logits, TOP_K)
    top_w = jax.nn.softmax(top_val, axis=-1)
    gates = jnp.einsum('tk,tke->te', top_w,
                       jax.nn.one_hot(top_idx, N_EXPERTS, dtype=jnp.float32)).astype(h.dtype)

    def expert(args):
        e_w1, e_w3, e_w2, g = args
        hid = jax.nn.silu(t @ e_w1) * (t @ e_w3)
        return (hid @ e_w2) * g[:, None]

    y = jnp.sum(lax.map(expert, (w1, w3, w2, gates.T)), axis=0)
    return y.reshape(b, s, d)

def second_inputs(seed: int = 0) -> dict:
    key = jax.random.key(seed)
    ks = jax.random.split(key, 14)
    nrm = lambda k, shape, fan_in: jax.random.normal(k, shape, jnp.float32) * fan_in ** -0.5
    x = jax.random.normal(ks[0], (BATCH, SEQ, D_MODEL), jnp.float32)
    w_qkv = nrm(ks[1], (DEPTH, D_MODEL, 3 * D_MODEL), D_MODEL)
    w_o = nrm(ks[2], (DEPTH, D_MODEL, D_MODEL), D_MODEL)
    mixer_norm = 1.0 + 0.02 * jax.random.normal(ks[3], (DEPTH, D_MODEL), jnp.float32)
    ffn_norm = 1.0 + 0.02 * jax.random.normal(ks[4], (DEPTH, D_MODEL), jnp.float32)
    rel_bias = 0.5 * jax.random.normal(ks[5], (N_BUCKETS, N_HEADS), jnp.float32)
    w1 = nrm(ks[6], (N_DENSE, D_MODEL, D_FF), D_MODEL)
    w3 = nrm(ks[7], (N_DENSE, D_MODEL, D_FF), D_MODEL)
    w2 = nrm(ks[8], (N_DENSE, D_FF, D_MODEL), D_FF)
    router = nrm(ks[9], (N_MOE, D_MODEL, N_EXPERTS), D_MODEL)
    e_w1 = nrm(ks[10], (N_MOE, N_EXPERTS, D_MODEL, D_FF_EXPERT), D_MODEL)
    e_w3 = nrm(ks[11], (N_MOE, N_EXPERTS, D_MODEL, D_FF_EXPERT), D_MODEL)
    e_w2 = nrm(ks[12], (N_MOE, N_EXPERTS, D_FF_EXPERT, D_MODEL), D_FF_EXPERT)
    final_norm = 1.0 + 0.02 * jax.random.normal(ks[13], (D_MODEL,), jnp.float32)
    return {'x': x, 'w_qkv': w_qkv, 'w_o': w_o, 'mixer_norm': mixer_norm,
            'ffn_norm': ffn_norm, 'rel_bias': rel_bias, 'w1': w1, 'w3': w3, 'w2': w2,
            'router': router, 'e_w1': e_w1, 'e_w3': e_w3, 'e_w2': e_w2,
            'final_norm': final_norm}

def second_block(x, w_qkv, w_o, mixer_norm, ffn_norm, rel_bias, w1, w3, w2,
              router, e_w1, e_w3, e_w2, final_norm):
    b, s, d = x.shape
    h = x
    for i in range(DEPTH):
        hn = rmsnorm(h, mixer_norm[i])
        q, k, v = qkv_heads(hn, w_qkv[i])
        if i % 2 == 0:
            o = stick_breaking_attention(q, k, v)
        else:
            o = moba_attention(q, k, v, rel_bias)
        o = o.transpose(0, 2, 1, 3).reshape(b, s, d)
        h = h + jnp.einsum('bsd,de->bse', o, w_o[i])
        hn = rmsnorm(h, ffn_norm[i])
        j = i // 2
        if i % 2 == 0:
            h = h + swiglu(hn, w1[j], w3[j], w2[j])
        else:
            h = h + moe_swiglu(hn, router[j], e_w1[j], e_w3[j], e_w2[j])
    return rmsnorm(h, final_norm)


def setup_inputs(seed=0):
    out = dict(first_inputs(seed))
    for name, value in second_inputs(seed + 1).items():
        if name != "x":
            out[name + "_2"] = value
    return out


def reference(
    x, c, ctx, c_ctx, norm_g, w_mod, b_mod, a_w_in, a_q_norm_g, a_k_norm_g, a_w_out, b_w_in,
    b_rpb, b_w_out, final_norm_g, w_qkv_2, w_o_2, mixer_norm_2, ffn_norm_2, rel_bias_2, w1_2,
    w3_2, w2_2, router_2, e_w1_2, e_w3_2, e_w2_2, final_norm_2,
):
    x = first_block(
        x, c, ctx, c_ctx, norm_g, w_mod, b_mod, a_w_in, a_q_norm_g, a_k_norm_g, a_w_out, b_w_in,
        b_rpb, b_w_out, final_norm_g,
    )
    return second_block(
        x, w_qkv_2, w_o_2, mixer_norm_2, ffn_norm_2, rel_bias_2, w1_2, w3_2, w2_2, router_2,
        e_w1_2, e_w3_2, e_w2_2, final_norm_2,
    )


_drawn_inputs = setup_inputs


def setup_inputs(seed=0):
    import zlib

    import numpy as np

    out = dict(_drawn_inputs(seed))
    spreads = {}
    factors = {'norm_g': 8.0,
     'a_q_norm_g': 4.456,
     'a_k_norm_g': 8.0,
     'b_rpb': 34.095,
     'final_norm_2': 7.937}
    for name, (base, spread) in spreads.items():
        noise = np.random.default_rng([zlib.crc32(name.encode()), seed]).standard_normal(out[name].shape)
        drawn = base * np.exp(spread * noise) if base else spread * noise
        out[name] = __import__('jax').numpy.asarray(drawn.astype(out[name].dtype))
    for name, factor in factors.items():
        out[name] = (out[name] * factor).astype(out[name].dtype)
    return out
```

```python
from contextlib import ExitStack

import numpy as np
import concourse.bass as bass
from concourse import mybir

ALU = mybir.AluOpType
ACT = mybir.ActivationFunctionType
AX = mybir.AxisListType
F32 = mybir.dt.float32
F32R = mybir.dt.float32r
I32 = mybir.dt.int32
U32 = mybir.dt.uint32

P = 128
D = 1024
CH = D // P
TOK = 256
TT = TOK // P
HEADS, HD = 16, 64
PAIRS = HEADS // 2
KVH = 4
GRID_W = 64
GROWS = TOK // GRID_W
RPB_R, RPB_C = 15, 31
BUCKETS = 32
FF = 2816
EXP, FE = 8, 3584
UW = 2048
NRAW, NSPLIT = 3, 3
NEG = -1e30
EPS = 1e-6
T5W = 384
HF = FF // 256
MAXOVER = 3
UV = 42

V_NORM, V_BMOD, V_MIX, V_FFN, V_C = 0, 16, 64, 80, 96
NVEC = 112


def shape_constants():
    f = np.float32
    tok = np.arange(TOK)
    inv = f(10000.0) ** (-np.arange(0, 32, 2, dtype=f) / f(32))
    ang = np.stack([(tok // GRID_W).astype(f)[:, None] * inv, (tok % GRID_W).astype(f)[:, None] * inv], 1)
    cos, sin = np.cos(ang), np.sin(ang)
    cos64 = np.stack([cos, cos], 2).reshape(TT, P, HD)
    sin64 = np.stack([-sin, sin], 2).reshape(TT, P, HD)
    q, k = np.arange(P)[:, None], np.arange(P)[None, :]
    col = GRID_W - 1 - np.arange(P) % GRID_W
    c0 = np.clip(col - 8, 0, GRID_W - 16)[:, None]
    kc = np.arange(GRID_W)[None, :]
    near = np.where((kc >= c0) & (kc < c0 + 16), 0.0, NEG)
    strict = (k < q).astype(f)
    causal = np.concatenate([np.where(k <= P - 1 - q, 0.0, NEG),
                             np.where(np.arange(TOK)[None, :] <= TOK - 1 - q, 0.0, NEG)], 1)
    keep = np.concatenate([np.eye(P), near, strict, np.where(strict > 0, 0.0, NEG), causal], 1).astype(f)
    once = np.concatenate([cos64[0], cos64[1], sin64[0], sin64[1]], 1).astype(f)
    n = np.maximum(TOK - 1 - np.arange(T5W), 0)
    large = 16 + (np.log(np.maximum(n, 1).astype(f) / f(16)) / f(np.log(8.0)) * f(16)).astype(np.int32)
    bucket = np.where(n < 16, n, np.minimum(large, BUCKETS - 1))
    onehot = (bucket[None, :] == np.arange(BUCKETS)[:, None]).astype(f)
    route = np.concatenate([(q < k).astype(f), np.broadcast_to(k, (P, P)).astype(f)], 1)
    return keep, once, onehot, np.ascontiguousarray(route)


K_ID, K_NEAR, K_STRICT, K_NEGS, K_CAUSAL, K_END = 0, 128, 192, 320, 448, 832


def build(nc, A, out, dbg=None, stop=None):
    scratch = nc.dram_tensor("t5_rows", [HEADS, T5W], F32, kind="Internal").ap()
    a_w_in, a_w_out = A["a_w_in"][0], A["a_w_out"][0]
    b_w_in, b_w_out = A["b_w_in"][0], A["b_w_out"][0]
    w_mod, w_qkv, w_o = A["w_mod"], A["w_qkv_2"], A["w_o_2"]
    ff1, ff3, ff2 = A["w1_2"][0], A["w3_2"][0], A["w2_2"][0]
    router = A["router_2"][0]

    units, first = [], {}

    def columns(name, w):
        first[name] = len(units)
        for c0 in range(0, w.shape[1], 512):
            for r0 in range(0, D, 512):
                units.append((w[r0:r0 + 512, c0:c0 + 512].rearrange("(c p) n -> p c n", p=P), 4))

    columns("mod0", w_mod[0])
    columns("mod1", w_mod[1])
    NMOD = len(units)
    columns("a_in", a_w_in)
    columns("a_out", a_w_out)
    columns("b_in", b_w_in)
    columns("b_out", b_w_out)
    columns("qkv0", w_qkv[0])
    columns("o0", w_o[0])
    first["ff"] = len(units)
    ff_at = {}

    def ff_unit(kind, j):
        ff_at[kind, j] = len(units) - NMOD
        if kind == 2:
            units.append((ff2[j * 256:(j + 1) * 256, :].rearrange("(c p) n -> p c n", p=P), 2))
        else:
            w = ff1 if kind == 1 else ff3
            units.append((w[:, j * 256:(j + 1) * 256].rearrange("(c p) n -> p c n", p=P), 8))

    for j in range(HF):
        ff_unit(1, j)
        ff_unit(3, j)
        if j:
            ff_unit(2, j - 1)
    ff_unit(2, HF - 1)
    columns("qkv1", w_qkv[1])
    columns("o1", w_o[1])
    NU = len(units)
    NS = NU - NMOD
    at = {k: v - NMOD for k, v in first.items()}
    blocks_of = {"a_in": [4] * 5, "a_out": [4] * 2, "b_in": [4] * 8, "b_out": [2] * 2, "qkv0": [4, 4, 4, 4, 2, 2],
                 "o0": [2] * 2, "qkv1": [4, 4, 4, 4, 2, 2], "o1": [2] * 2}
    group_engine, group_at = [], {}
    used_by = [None] * NS
    single = 0
    for name in ("a_in", "a_out", "b_in", "b_out", "qkv0", "o0", "ff", "qkv1", "o1"):
        group_at[name] = len(group_engine)
        if name == "ff":
            for j in range(HF):
                for kind, who in ((1, "act"), (3, "dve")):
                    group_engine.append(who)
                    used_by[ff_at[kind, j]] = ("group_product_ready", len(group_engine))
                single += 1
                used_by[ff_at[2, j]] = ("w_used", single)
            continue
        for cb, n in enumerate(blocks_of[name]):
            single += 1
            group_engine += ["dve" if name[1:] in ("_out", "0", "1") else "act"] * n
            used_by[at[name] + 2 * cb] = ("w_used", single)
            used_by[at[name] + 2 * cb + 1] = ("group_product_ready", len(group_engine))
    last_unit = {k: at[k] + 2 * len(v) - 1 for k, v in blocks_of.items()}
    last_unit["ff"] = ff_at[2, HF - 1]

    def emptied_by(g):
        return group_engine[g], group_engine[:g + 1].count(group_engine[g])

    top = ExitStack()
    with top:
        semaphores = {}

        def sem(name):
            if name not in semaphores:
                semaphores[name] = top.enter_context(nc.semaphore(name))
            return semaphores[name]

        def sb(name, shape, dt=F32, ctx=top):
            return ctx.enter_context(nc.sbuf_tensor(name, shape, dt))

        bank = [top.enter_context(nc.psum_tensor(f"bank{i}", [P, 512], F32)) for i in range(8)]

        raw = sb("raw", [P, NRAW, UW])
        w_hi = sb("w_hi", [P, NSPLIT, UW], F32R)
        w_lo = sb("w_lo", [P, NSPLIT, UW], F32R)
        xs = sb("xs", [P, 2 * TT, D])
        ident = sb("ident", [P, K_END])
        near, strict = ident[:, K_NEAR:K_STRICT], ident[:, K_STRICT:K_NEGS]
        negstrict, causal = ident[:, K_NEGS:K_CAUSAL], ident[:, K_CAUSAL:K_END]
        eye = ident[:, 0:P]
        vec_t = sb("vec_t", [P, NVEC])
        ones = sb("ones", [P, TOK])
        stat = sb("stat", [P, 16])
        qk_root = sb("qk_root", [P, 8])
        minus_half = sb("minus_half", [P, 8])
        diag = sb("diag", [P, 2 * TT, P])

        gate_b = sb("gate_b", [P, 2, D])
        route = sb("route", [P, 2 * P])
        router_w = sb("router_w", [P, CH, EXP])

        ahead = ExitStack()
        h_hi = sb("h_hi", [P, CH, 2 * TOK], F32R, ahead)
        h_lo = sb("h_lo", [P, CH, 2 * TOK], F32R, ahead)
        prob = sb("prob", [P, 3, 512], F32, ahead)
        prob_t = sb("prob_t", [P, 2, 512], F32, ahead)
        work = sb("work", [P, 4, 512], F32, ahead)
        mod = sb("mod", [P, 2, 24, 2], F32, ahead)
        gain = sb("gain", [P, 2, CH, 2], F32, ahead)
        silu_c = sb("silu_c", [P, CH, 2], F32, ahead)
        negmax = sb("negmax", [P, 4, 4], F32, ahead)
        total = sb("total", [P, 4, 4], F32, ahead)
        inv = sb("inv", [P, 4, 4], F32, ahead)
        lay_a = ExitStack()
        ahead.enter_context(lay_a)
        q_a = sb("q_a", [P, PAIRS, 2 * TOK], F32, lay_a)
        k_a = sb("k_a", [P, KVH, 2 * TOK], F32, lay_a)
        v_a = sb("v_a", [P, 2 * TT, KVH * HD], F32, lay_a)
        z_a = sb("z_a", [P, CH, 2 * TOK], F32, lay_a)
        rope = sb("rope", [P, 4, TT, HD], F32, lay_a)
        qk_g = sb("qk_g", [P, 2, HD], F32, lay_a)
        lay_a.close()
        lay_b = ExitStack()
        q_b = sb("q_b", [P, PAIRS, TOK], F32, lay_b)
        k_b = sb("k_b", [P, PAIRS, 2 * TOK], F32, lay_b)
        v_b = sb("v_b", [P, 2 * TT, D], F32, lay_b)
        z_b = sb("z_b", [P, CH, TOK], F32, lay_b)
        bias_r = sb("bias_r", [P, 2, 2, TOK], F32, lay_b)
        lay_b.close()
        lay_2 = ExitStack()
        q_2 = sb("q_2", [P, PAIRS, TOK], F32, lay_2)
        k_2 = sb("k_2", [P, PAIRS, TOK], F32, lay_2)
        v_2 = sb("v_2", [P, TT, D], F32, lay_2)
        bias_t = sb("bias_t", [P, 2, T5W], F32, lay_2)
        hid_s = sb("hid_s", [P, 2, 512], F32, lay_2)
        hid_f = sb("hid_f", [P, 2, 512], F32, lay_2)
        hid_hi = sb("hid_hi", [P, 2, 512], F32R, lay_2)
        hid_lo = sb("hid_lo", [P, 2, 512], F32R, lay_2)
        lay_2.close()
        ahead.close()

        raw_x = sb("raw_x", [P, 3, UW])
        w_hi_x = sb("w_hi_x", [P, 3, UW], F32R)
        w_lo_x = sb("w_lo_x", [P, 3, UW], F32R)
        xe_hi = sb("xe_hi", [P, CH, P], F32R)
        xe_lo = sb("xe_lo", [P, CH, P], F32R)
        act_s = sb("act_s", [P, 512])
        act_f = sb("act_f", [P, 512])
        act_hi = sb("act_hi", [P, 512], F32R)
        act_lo = sb("act_lo", [P, 512], F32R)
        y_e = sb("y_e", [P, D])
        pick = sb("pick", [P, TT, P])
        pick_g = sb("pick_g", [P, TT, P])
        pick_gt = sb("pick_gt", [P, TOK])
        current = sb("current", [P, 6])
        visits = sb("visits", [P, EXP + MAXOVER + 1, 6])
        logit = sb("logit", [P, TT, EXP])
        best = sb("best", [P, TT, EXP])
        best_i = sb("best_i", [P, TT, EXP], U32)
        best_f = sb("best_f", [P, TT, 2])
        gates = sb("gates", [P, TT, 4])
        hot = sb("hot", [P, TT, 2, EXP])
        facts = sb("facts", [P, 6, EXP])
        over = sb("over", [P, 4, EXP])
        over_hot = sb("over_hot", [P, MAXOVER, EXP])
        over_tmp = sb("over_tmp", [P, MAXOVER, 6, EXP])
        ids_f = sb("ids_f", [P, 16])
        ids = sb("ids", [P, 16], I32)

        def ring6(base, more, n, a):
            ring = base if n % 6 < 3 else more
            return ring[:, n % 3, :].rearrange("p (a n) -> p a n", a=a)

        visit_units = []
        for j in range(FE // 512 + 1):
            if j < FE // 512:
                visit_units += [(1, j, 0), (1, j, 1), (3, j, 0), (3, j, 1)]
            if j:
                visit_units += [(2, j - 1, 0), (2, j - 1, 1)]
        NV = len(visit_units)
        unit_no = {u: k for k, u in enumerate(visit_units)}
        NJ = FE // 512

        def x_done_in(name):
            return emptied["dve"], emptied_by(group_at[name] + sum(blocks_of[name]) - 1)[1]

        def wait_used(eng, m):
            name, n = used_by[m]
            eng.wait_ge(sem(name), n)

        def unit_view(ring, n, a):
            return ring[:, n % NRAW, :].rearrange("p (a n) -> p a n", a=a)

        landed = [sem(f"weights_landed_{i}") for i in range(NRAW)]
        hi_ready, lo_ready, w_used = sem("w_hi_ready"), sem("w_lo_ready"), sem("w_used")
        mod_used = sem("mod_units_used")
        x_landed = [sem(f"expert_weights_landed_{i}") for i in range(6)]
        x_raw_free, x_split_free = sem("x_raw_free"), sem("x_split_free")
        x_hi_ready, x_lo_ready = sem("x_hi_ready"), sem("x_lo_ready")
        product = sem("group_product_ready")
        emptied = {"act": sem("bank_emptied_act"), "dve": sem("bank_emptied_dve")}

        def attention_plan():
            plans = {}
            ua = []
            for p in range(PAIRS):
                for t in range(TT):
                    for par in range(2):
                        ua.append((2 * p + par, [(t, t * P, 0, 2 * TOK, 0)], p))
            for p in range(PAIRS):
                for par in range(2):
                    ua.append((2 * p + par, [(t, TOK + t * P, TOK, TOK, t * TOK) for t in range(TT)], PAIRS + p))
            plans["a"] = ua
            plans["b"] = [u for u in ua if u[2] < PAIRS]
            plans["s"] = [(h, [(0, 0, 0, P, 0), (1, P, 0, TOK, P)], h // 2) for h in range(HEADS)]
            plans["m"] = plans["s"]
            return plans

        plans = attention_plan()
        LAG = {"a": 2, "b": 2, "s": 3, "m": 2}

        def query_operand(st, h, q0):
            par = h % 2 * HD
            return {"a": q_a, "b": q_b}.get(st, q_2)[par:par + HD, h // 2, q0:q0 + P]

        def key_operand(st, h, k0, n):
            par = h % 2 * HD
            if st == "a":
                return k_a[par:par + HD, h // 4, k0:k0 + n]
            return (k_b if st == "b" else k_2)[par:par + HD, h // 2, k0:k0 + n]

        def value_operand(st, h, chunk):
            if st == "a":
                return v_a[:, chunk, h // 4 * HD:h // 4 * HD + HD]
            return (v_b if st == "b" else v_2)[:, chunk, h * HD:h * HD + HD]

        norm_tiles = {"n0": 4, "n1": 4, "f1": 2, "n2": 2, "n3": 2, "n4": 2, "n5": 2, "n6": 2}
        whole = ("n0", "n1", "n2", "n3", "n4")
        signals = {"squares": norm_tiles, "mean": {st: 1 for st in norm_tiles}, "root": {st: 1 for st in norm_tiles},
                   "diag": {st: norm_tiles[st] for st in whole}}
        for role in ("transposed", "h_full", "h_hi", "h_lo"):
            signals[role] = {st: CH for st in whole}
        for role in ("negmax", "exp"):
            signals[role] = {st: len(plans[st]) for st in "abm"}
        for role in ("scores", "prob", "prob_turned", "prob_t", "mixed"):
            signals[role] = {st: len(plans[st]) for st in "absm"}
        for role in ("gated", "out_hi", "out_lo"):
            signals[role] = {st: plans[st][-1][2] + 1 for st in "absm"}
        stage_sem = {role: sem(role) for role in signals}

        def reached(st, role, n):
            stages = list(signals[role])
            return stage_sem[role], sum(signals[role][s] for s in stages[:stages.index(st)]) + n

        S_BANK, T_BANK, O_BANK = [4, 5, 6, 3], [7, 0], [1, 2]

        def group_ends(st):
            u = plans[st]
            return {i: u[i][2] for i in range(len(u)) if i + 1 == len(u) or u[i + 1][2] != u[i][2]}

        def group_starts(st):
            u = plans[st]
            return {i: u[i][2] for i in range(len(u)) if i == 0 or u[i - 1][2] != u[i][2]}

        block = top.enter_context(nc.Block())
        done = lambda name: stop == name

        @block.sync
        def _(sp):
            def load_unit(n):
                ap, a = units[n]
                if n >= NRAW:
                    m = n - NRAW
                    if m < NMOD:
                        sp.wait_ge(mod_used, m + 1)
                    else:
                        sp.wait_ge(lo_ready, m - NMOD + 1)
                sp.dma_start(unit_view(raw, n, a), ap).then_inc(landed[n % NRAW], 16)

            def load_near_bias():
                rpb = A["b_rpb"].tensor
                for h in range(HEADS):
                    if h >= 2:
                        sp.wait_ge(sem("b_bias_used"), 4 * (h // 2 - 1) + 3 + h % 2)
                    for t in range(TT):
                        for half in range(2):
                            r = 2 * t + 1 - half
                            src = bass.AP(rpb, h * RPB_R * RPB_C + (7 - r) * RPB_C + 15 - (GRID_W - 1),
                                          [[1, GRID_W], [RPB_C, GROWS], [1, GRID_W]])
                            dst = bias_r[half * GRID_W:(half + 1) * GRID_W, h % 2, t, :]
                            sp.dma_start(dst.rearrange("p (r c) -> p r c", r=GROWS), src)\
                              .then_inc(sem(f"near_bias_landed_{h % 2}"), 16)

            def load_t5_bias():
                sp.wait_ge(sem("t5_rows_stored"), 16)
                for h in range(HEADS):
                    if h >= 2:
                        sp.wait_ge(sem("m_bias_used"), h - 1)
                    for t, c0, n in ((0, 0, P), (1, P, TOK)):
                        src = bass.AP(scratch.tensor, h * T5W + P * (1 - t), [[1, P], [1, n]])
                        sp.dma_start(bias_t[:, h % 2, c0:c0 + n], src).then_inc(sem(f"t5_bias_landed_{h % 2}"), 16)

            for n in range(NU):
                if (done("a") and n == first["b_in"] + 2) or (done("b") and n == first["qkv0"] + 2):
                    break
                if n == first["b_out"] + 3:
                    wait_used(sp, last_unit["b_in"])
                    load_near_bias()
                if n == first["o1"] + 3:
                    wait_used(sp, last_unit["qkv1"])
                    load_t5_bias()
                load_unit(n)
            if stop:
                sp.wait_ge(sem({"a": "a_x_done", "b": "b_x_done", "f": "bank_emptied_dve"}[stop]), {"a": 8, "b": 4, "f": x_done_in("o1")[1]}[stop])
                sp.dma_start(out[0].rearrange("(t p) d -> p t d", p=P), xs[:, 0:TT, :]).then_inc(sem("stored"), 16)
                sp.wait_ge(sem("stored"), 16)
                return

            def load_expert(v, e):
                for k, (kind, j, half) in enumerate(visit_units):
                    if kind == 2:
                        src = A["e_w2_2"][0, e, j * 512:(j + 1) * 512, half * 512:(half + 1) * 512]
                    else:
                        src = A["e_w1_2" if kind == 1 else "e_w3_2"][0, e, half * 512:(half + 1) * 512, j * 512:(j + 1) * 512]
                    src = src.rearrange("a (c p) n -> p (a c) n", p=P) if len(src.shape) == 3 else src.rearrange("(c p) n -> p c n", p=P)
                    sp.wait_ge(x_raw_free, v * NV + k + 1)
                    sp.dma_start(ring6(raw, raw_x, k, 4), src).then_inc(x_landed[k % 6], 16)

            load_expert(0, 0)
            sp.wait_ge(sem("routed"), 1)
            n_visits = sp.value_load(ids[0:1, 12:13], min_val=EXP, max_val=EXP + MAXOVER)
            with sp.Fori(1, n_visits) as v:
                e = sp.value_load(ids[0:1, bass.ds(v, 1)], min_val=0, max_val=EXP - 1)
                load_expert(v, bass.ds(e, 1))
            sp.wait_ge(sem("y_done"), TT)
            sp.dma_start(out[0].rearrange("(t p) d -> p t d", p=P), xs[:, TT:2 * TT, :]).then_inc(sem("stored"), 16)
            sp.wait_ge(sem("stored"), 16)

        @block.scalar
        def _(act):
            state = {"split": 0}

            def load(dst, src, name, n=16):
                act.dma_start(dst, src).then_inc(sem(name), n)

            vec = work[:, 0, 0:P]
            rows = [(V_NORM, A["norm_g"].rearrange("l (c p) -> (l c) p", p=P)),
                    (V_BMOD, A["b_mod"].rearrange("l (c p) -> (l c) p", p=P)),
                    (V_MIX, A["mixer_norm_2"].rearrange("l (c p) -> (l c) p", p=P)),
                    (V_FFN, A["ffn_norm_2"].rearrange("l (c p) -> (l c) p", p=P)),
                    (V_C, A["c"].rearrange("l (c p) -> (l c) p", p=P)),
                    (V_C + CH, A["c_ctx"].rearrange("(c p) -> c p", p=P))]
            for r0, src in rows:
                load(vec[r0:r0 + src.shape[0], :], src, "vectors_landed")
            load(ident[:], A["keep"], "constants_landed")
            load(work[:, 1, 0:4 * HD], A["once"], "constants_landed")
            load(work[0:BUCKETS, 2, 0:T5W], A["onehot"], "t5_landed")
            load(work[0:BUCKETS, 3, 0:HEADS], A["rel_bias_2"], "t5_landed")
            load(qk_g[:, 0, :], bass.AP(A["a_q_norm_g"].tensor, 0, [[0, P], [1, HD]]), "qk_gain_landed")
            load(qk_g[:, 1, :], bass.AP(A["a_k_norm_g"].tensor, 0, [[0, P], [1, HD]]), "qk_gain_landed")
            load(xs[:, 0:TT, :], A["x"][0].rearrange("(t p) d -> p t d", p=P), "x_landed")
            load(xs[:, TT:2 * TT, :], A["ctx"][0].rearrange("(t p) d -> p t d", p=P), "x_landed")

            def split(upto):
                while state["split"] < min(upto, NS):
                    m = state["split"]
                    n = m + NMOD
                    act.wait_ge(landed[n % NRAW], 16 * (n // NRAW + 1))
                    if m >= NSPLIT:
                        wait_used(act, m - NSPLIT)
                    nc.scalar.activation(w_hi[:, m % NSPLIT, :], raw[:, n % NRAW, :], ACT.Copy).then_inc(hi_ready, 1)
                    state["split"] += 1

            act.wait_ge(sem("t5_rows"), 1)
            nc.scalar.activation(prob[0:HEADS, 0, 0:T5W], bank[7][0:HEADS, 0:T5W], ACT.Copy).then_inc(sem("t5_copied"), 1)
            act.wait_ge(sem("t5_copied"), 1)
            act.dma_start(scratch, prob[0:HEADS, 0, 0:T5W]).then_inc(sem("t5_rows_stored"), 16)
            act.wait_ge(sem("vec_t_ready"), 1)
            nc.scalar.activation(silu_c[:].rearrange("p c w -> p w c"),
                                 vec_t[:, V_C:V_C + 2 * CH].rearrange("p (w c) -> p w c", w=2),
                                 ACT.Silu).then_inc(sem("silu_c_ready"), 1)

            def norm(st, tiles, x_done, read_before):
                act.wait_ge(*x_done)
                act.wait_ge(sem("t5_rows_stored"), 16)
                for t in range(tiles):
                    if t:
                        act.wait_ge(*reached(st, "squares", t))
                    nc.scalar.activation(prob[:, 0:2, :].rearrange("p a n -> p (a n)"), xs[:, t, :], ACT.Square,
                                         accum_out=stat[:, t:t + 1]).then_inc(stage_sem["squares"], 1)
                if read_before is not None:
                    wait_used(act, read_before)
                for c in range(CH):
                    act.wait_ge(*reached(st, "h_full", c + 1))
                    nc.scalar.activation(h_hi[:, c, 0:tiles * P], work[:, c % 2, 0:tiles * P], ACT.Copy).then_inc(stage_sem["h_hi"], 1)

            def linear(name, blocks, per_block, evac, after=None):
                g0 = group_at[name]
                for cb in range(blocks):
                    split(at[name] + 2 * cb + 4)
                    for i in range(per_block[cb]):
                        g = g0 + sum(per_block[:cb]) + i
                        act.wait_ge(product, g + 1)
                        evac(cb, i, bank[g % 4]).then_inc(emptied["act"], 1)
                    if after:
                        after(cb)

            def attention(st):
                plan, lag = plans[st], LAG[st]
                ends, n = group_ends(st), len(plan)
                for i in range(n + lag + 3):
                    if i < n:
                        h, segs, _ = plan[i]
                        s = bank[S_BANK[i % 4]]
                        if st != "s" and i >= 3:
                            act.wait_ge(*reached(st, "prob_turned", i - 2))
                        if st == "s":
                            w = T5W
                            act.wait_ge(*reached("s", "scores", i + 1))
                            if i >= 2:
                                act.wait_ge(sem("s_softplus"), i - 1)
                            a = work[:, i % 2, 0:w]
                            nc.scalar.activation(a, s[:, 0:w], ACT.Abs).then_inc(sem("s_abs"), 1)
                            act.wait_ge(sem("s_abs"), i + 1)
                            nc.scalar.activation(a, a, ACT.Exp, scale=-1.0).then_inc(sem("s_exp_abs"), 1)
                            act.wait_ge(sem("s_exp_abs"), i + 1)
                            nc.scalar.activation(a, a, ACT.Ln, bias=1.0).then_inc(sem("s_log1p"), 1)
                        else:
                            act.wait_ge(*reached(st, "negmax", i + 1))
                            for j, (t, q0, k0, nk, c0) in enumerate(segs):
                                last = nc.scalar.activation(prob[:, i % 3, c0:c0 + nk], s[:, c0:c0 + nk], ACT.Exp,
                                                            bias=negmax[:, i % 4, j:j + 1],
                                                            accum_out=total[:, i % 4, j:j + 1])
                            last.then_inc(stage_sem["exp"], 1)
                    if st == "s" and 1 <= i <= n:
                        act.wait_ge(sem("s_log_weight"), i)
                        nc.scalar.activation(prob[:, (i - 1) % 3, 0:T5W], prob[:, (i - 1) % 3, 0:T5W],
                                             ACT.Exp).then_inc(stage_sem["prob"], 1)
                    u = i - lag
                    if 0 <= u < n:
                        w = sum(x[3] for x in plan[u][1])
                        act.wait_ge(*reached(st, "prob_turned", u + 1))
                        if u >= 2:
                            act.wait_ge(*reached(st, "mixed", u - 1))
                        nc.scalar.activation(prob_t[:, u % 2, 0:w], bank[T_BANK[u % 2]][:, 0:w], ACT.Copy)\
                          .then_inc(stage_sem["prob_t"], 1)
                    u = i - lag - 2
                    if u in ends:
                        p = ends[u]
                        act.wait_ge(*reached(st, "gated", p + 1))
                        nc.scalar.activation(out_hi(p, h_hi), gated_slot(p), ACT.Copy).then_inc(stage_sem["out_hi"], 1)

            norm("n0", 4, (sem("x_landed"), 32), None)

            def evac_a(cb, i, b):
                if cb < 3:
                    j = 4 * cb + i
                    if j >= 3:
                        act.wait_ge(sem("a_qk_normed"), j - 2)
                    if cb < 2:
                        return nc.scalar.activation(prob[:, j % 3, :], b[:], ACT.Copy)
                    nc.scalar.activation(v_a[:, i, :], b[:, 256:512], ACT.Copy)
                    return nc.scalar.activation(prob[:, j % 3, 0:256], b[:, 0:256], ACT.Copy)
                return nc.scalar.activation(z_a[:, (cb - 3) * 4 + i, :], b[:], ACT.Silu)

            def turn_a(cb):
                if 1 <= cb <= 3:
                    for tt in range(4):
                        j = 4 * (cb - 1) + tt
                        act.wait_ge(sem("a_qk_turned"), j + 1)
                        src = bank[4 + j % 4][:].rearrange("p (c t) -> p c t", c=4)
                        cols = slice(tt * P, (tt + 1) * P)
                        if cb - 1 < 2:
                            last = nc.scalar.activation(q_a[:, (cb - 1) * 4:cb * 4, cols], src, ACT.Copy, scale=HD ** -0.5)
                        else:
                            last = nc.scalar.activation(k_a[:, :, cols], src, ACT.Copy)
                        last.then_inc(sem("a_qk_kept"), 1)

            def gated_slot(p):
                return work[:, 2 + p % 2, 0:TOK]

            def out_hi(p, ring):
                return ring[:, p % PAIRS, p // PAIRS * TOK:(p // PAIRS + 1) * TOK]

            def gate_rows(n0, n1):
                for n in range(n0, n1):
                    act.wait_ge(sem("gate_spread"), 4 * (n + 1))
                    nc.scalar.activation(gate_b[:, n // 2 % 2, n % 2 * 512:(n % 2 + 1) * 512], bank[4 + n % 4][:], ACT.Copy)\
                      .then_inc(sem("gate_copied"), 1)

            linear("a_in", 5, [4] * 5, evac_a, turn_a)
            gate_rows(0, 4)
            attention("a")
            split(at["a_out"] + 4)
            split(at["b_in"] + 2)
            if done("a"):
                return

            norm("n1", 4, (sem("a_x_done"), 8), last_unit["a_out"])

            def flipped(b):
                return b[:, 0:TOK].rearrange("p (t n) -> p t n", t=TT)[:, :, ::-1]

            def evac_b(cb, i, b):
                c = cb % 2 * 4 + i
                if cb < 2:
                    return nc.scalar.activation(q_b[:, c, :].rearrange("p (t n) -> p t n", t=TT), flipped(b),
                                                ACT.Copy, scale=HD ** -0.5)
                if cb < 4:
                    return nc.scalar.activation(k_b[:, c, :], b[:], ACT.Copy)
                if cb < 6:
                    return nc.scalar.activation(v_b[:, i, (cb - 4) * 512:(cb - 3) * 512], b[:], ACT.Copy)
                return nc.scalar.activation(z_b[:, c, :], b[:, 0:TOK], ACT.Silu)

            linear("b_in", 8, [4] * 8, evac_b)
            gate_rows(4, 6)
            attention("b")
            split(at["b_out"] + 4)
            split(at["qkv0"] + 2)
            if done("b"):
                return
            act.wait_ge(sem("b_x_done"), 4)
            for t in range(TT):
                if t:
                    act.wait_ge(*reached("f1", "squares", t))
                nc.scalar.activation(prob[:, 0:2, :].rearrange("p a n -> p (a n)"), xs[:, t, :], ACT.Square,
                                     accum_out=stat[:, t:t + 1]).then_inc(stage_sem["squares"], 1)

            def evac_qkv(flip):
                def evac(cb, i, b):
                    c = cb % 2 * 4 + i
                    if cb < 2:
                        src = flipped(b) if flip else b[:, 0:TOK].rearrange("p (t n) -> p t n", t=TT)
                        return nc.scalar.activation(q_2[:, c, :].rearrange("p (t n) -> p t n", t=TT), src,
                                                    ACT.Copy, scale=HD ** -0.5)
                    if cb < 4:
                        return nc.scalar.activation(k_2[:, c, :], b[:, 0:TOK], ACT.Copy)
                    return nc.scalar.activation(v_2[:, i, (cb - 4) * 512:(cb - 3) * 512], b[:], ACT.Copy)
                return evac

            norm("n2", 2, (sem("f1_x_done"), 2), last_unit["b_out"])
            linear("qkv0", 6, [4, 4, 4, 4, 2, 2], evac_qkv(False))
            attention("s")
            split(at["o0"] + 4)
            split(at["ff"] + 2)
            norm("n3", 2, x_done_in("o0"), last_unit["o0"])
            g0 = group_at["ff"]
            for j in range(HF):
                split(ff_at[1, j] + 3)
                act.wait_ge(product, g0 + 2 * j + 1)
                if j >= 2:
                    act.wait_ge(emptied["dve"], emptied_by(g0 + 2 * j - 3)[1])
                nc.scalar.activation(hid_s[:, j % 2, :], bank[(g0 + 2 * j) % 4][:], ACT.Silu).then_inc(emptied["act"], 1)
                split(ff_at[3, j] + 3)
                act.wait_ge(emptied["dve"], emptied_by(g0 + 2 * j + 1)[1])
                if j >= 2:
                    wait_used(act, ff_at[2, j - 2])
                nc.scalar.activation(hid_hi[:, j % 2, :], hid_f[:, j % 2, :], ACT.Copy).then_inc(sem("ff_hid_hi"), 1)
                split(ff_at[1, min(j + 1, HF - 1)] + 2)
            split(at["qkv1"] + 2)
            norm("n4", 2, (sem("ff_x_done"), 4), last_unit["ff"])
            linear("qkv1", 6, [4, 4, 4, 4, 2, 2], evac_qkv(True))
            split(NS - 1)
            attention("m")
            split(NS)
            if done("f"):
                return

            def squares(st, tiles):
                for t in range(tiles):
                    if t:
                        act.wait_ge(*reached(st, "squares", t))
                    nc.scalar.activation(y_e[:], xs[:, t, :], ACT.Square, accum_out=stat[:, t:t + 1]).then_inc(stage_sem["squares"], 1)

            act.wait_ge(*x_done_in("o1"))
            squares("n5", TT)
            for t in range(TT):
                for half in range(2):
                    act.wait_ge(sem("n5_turned"), 2 * t + half + 1)
                    nc.scalar.activation(y_e[:, half * 512:(half + 1) * 512], bank[6 + half][:], ACT.Copy).then_inc(sem("n5_turned_kept"), 1)
            act.wait_ge(sem("gap_ready"), 1)
            nc.scalar.activation(gates[:, :, 1], gates[:, :, 0], ACT.Exp).then_inc(sem("gap_exp"), 1)

            def gathered(n):
                for b in range(2):
                    act.wait_ge(sem("x_gathered"), 2 * n + b - 1)
                    nc.scalar.activation(xe_hi[:, 4 * b:4 * b + 4, :].rearrange("p c s -> p (c s)"), bank[6 + b][:], ACT.Copy)\
                      .then_inc(sem("xe_hi_ready"), 1)

            gathered(1)
            act.wait_ge(sem("routed"), 1)
            n_visits = act.value_load(ids[0:1, 12:13], min_val=EXP, max_val=EXP + MAXOVER)
            with act.Fori(0, n_visits) as v:
                def round_unit(k):
                    act.wait_ge(x_landed[k % 6], v * (16 * NV // 6) + 16 * (k // 6 + 1))
                    act.wait_ge(x_split_free, v * NV + k + 1)
                    nc.scalar.activation(ring6(w_hi, w_hi_x, k, 1)[:, 0, :], ring6(raw, raw_x, k, 1)[:, 0, :], ACT.Copy).then_inc(x_hi_ready, 1)

                def turned(j):
                    act.wait_ge(sem("x_turned"), v * NJ + j + 1)
                    nc.scalar.activation(act_hi[:], bank[2][:], ACT.Copy).then_inc(sem("act_hi_ready"), 1)

                for k in range(6):
                    round_unit(k)
                for k, (kind, j, half) in enumerate(visit_units):
                    if half:
                        if kind == 1:
                            act.wait_ge(x_split_free, v * NV + k + 7)
                            if j:
                                act.wait_ge(sem("act_f_ready"), v * NJ + j)
                            nc.scalar.activation(act_s[:], bank[0][:], ACT.Silu).then_inc(sem("act_s_ready"), 1)
                            if j:
                                turned(j - 1)
                            if j == 2:
                                act.wait_ge(sem("pick_turned"), v + 1)
                                nc.scalar.activation(pick_gt[:], bank[3][:, 0:TOK], ACT.Copy).then_inc(sem("pick_gt_ready"), 1)
                        if kind == 2 and j == NJ - 2:
                            gathered(v + 2)
                            turned(NJ - 1)
                        if kind == 2 and j == NJ - 1:
                            act.wait_ge(x_split_free, v * NV + NV + 6)
                            for b in range(2):
                                nc.scalar.activation(y_e[:, b * 512:(b + 1) * 512], bank[4 + b][:], ACT.Copy).then_inc(sem("y_ready"), 1)
                    if k + 6 < NV:
                        round_unit(k + 6)

            act.wait_ge(sem("x_added"), n_visits * 4 + 4)
            squares("n6", TT)

        @block.vector
        def _(dve):
            state = {"split": 0}
            last_count = {}

            def then(ins, name):
                last_count[name] = last_count.get(name, 0) + 1
                ins.then_inc(sem(name), 1)
                dve.wait_ge(sem(name), last_count[name])

            def split(upto):
                while state["split"] < min(upto, NS):
                    m = state["split"]
                    dve.wait_ge(hi_ready, m + 1)
                    nc.vector.tensor_tensor(w_lo[:, m % NSPLIT, :], raw[:, (m + NMOD) % NRAW, :],
                                            w_hi[:, m % NSPLIT, :].bitcast(F32), ALU.subtract).then_inc(lo_ready, 1)
                    state["split"] += 1

            nc.vector.memset(ones[:], 1.0).then_inc(sem("ones_ready"), 1)
            nc.vector.memset(minus_half[:], -0.5).then_inc(sem("ones_ready"), 1)
            dve.wait_ge(sem("vec_turned"), 1)
            nc.vector.tensor_copy(vec_t[:], bank[6][:, 0:NVEC]).then_inc(sem("vec_t_ready"), 1)
            dve.wait_ge(sem("vec_t_ready"), 1)
            dve.wait_ge(sem("constants_landed"), 32)
            dve.wait_ge(sem("qk_gain_landed"), 32)
            for w in range(2):
                for t in range(TT):
                    cos = work[:, 1, t * HD:(t + 1) * HD]
                    sin = work[:, 1, (TT + t) * HD:(TT + t + 1) * HD]
                    nc.vector.tensor_tensor(rope[:, 2 * w, t, :], cos, qk_g[:, w, :], ALU.mult)
                    g4 = qk_g[:, w, :].rearrange("p (a h i) -> p a h i", a=2, h=2)
                    s4 = sin.rearrange("p (a h i) -> p a h i", a=2, h=2)
                    o4 = rope[:, 2 * w + 1, t, :].rearrange("p (a h i) -> p a h i", a=2, h=2)
                    for half in range(2):
                        last = nc.vector.tensor_tensor(o4[:, :, half, :], s4[:, :, half, :], g4[:, :, 1 - half, :], ALU.mult)
            last.then_inc(sem("rope_ready"), 1)

            for l in range(2):
                for cb in range(6):
                    dve.wait_ge(mod_used, 2 * (6 * l + cb) + 2)
                    for i in range(4):
                        m = 4 * cb + i
                        b_col = vec_t[:, V_BMOD + 24 * l + m:V_BMOD + 24 * l + m + 1]
                        last = nc.vector.tensor_scalar(mod[:, l, m, :], bank[4 * (cb % 2) + i][:, 0:2],
                                                       b_col, None, ALU.add)
                    last.then_inc(sem("mod_ready"), 1)
                dve.wait_ge(sem("mod_ready"), 6 * l + 6)
                for w in range(2):
                    last = nc.vector.scalar_tensor_tensor(gain[:, l, :, w], mod[:, l, CH:2 * CH, w], 1.0,
                                                          vec_t[:, V_NORM + CH * l:V_NORM + CH * (l + 1)], ALU.add, ALU.mult)
                last.then_inc(sem("gain_ready"), 1)
            dve.wait_ge(sem("gain_ready"), 2)

            def roots(st, tiles):
                dve.wait_ge(*reached(st, "squares", tiles))
                v, r = stat[:, 4:4 + tiles], stat[:, 8:8 + tiles]
                nc.vector.tensor_scalar(v, stat[:, 0:tiles], 1.0 / D, EPS, ALU.mult, ALU.add).then_inc(stage_sem["mean"], 1)
                dve.wait_ge(*reached(st, "root", 1))
                return r

            def norm(st, tiles, scale, shift, read_before):
                r = roots(st, tiles)
                for t in range(tiles):
                    nc.vector.tensor_scalar(diag[:, t, :], eye, r[:, t:t + 1], None, ALU.mult).then_inc(stage_sem["diag"], 1)
                if read_before is not None:
                    wait_used(dve, read_before)
                width = tiles * P

                def rest(c):
                    dve.wait_ge(*reached(st, "h_hi", c + 1))
                    dve.wait_ge(*reached(st, "h_full", c + 1))
                    nc.vector.tensor_tensor(h_lo[:, c, 0:width], work[:, c % 2, 0:width],
                                            h_hi[:, c, 0:width].bitcast(F32), ALU.subtract).then_inc(stage_sem["h_lo"], 1)

                for c in range(CH):
                    dve.wait_ge(*reached(st, "transposed", c + 1))
                    if c >= 2:
                        dve.wait_ge(*reached(st, "h_lo", c - 1))
                    for w in range(tiles // TT):
                        cols = slice(w * TOK, (w + 1) * TOK)
                        if shift:
                            last = nc.vector.tensor_scalar(work[:, c % 2, cols], bank[4 + c % 4][:, cols], scale(c, w),
                                                           shift(c, w), ALU.mult, ALU.add)
                        else:
                            last = nc.vector.tensor_scalar(work[:, c % 2, cols], bank[4 + c % 4][:, cols], scale(c, w),
                                                           None, ALU.mult)
                    last.then_inc(stage_sem["h_full"], 1)
                    if c:
                        rest(c - 1)
                rest(CH - 1)

            def gate_rows(l, w, k):
                for c in range(CH):
                    i = k * CH + c
                    if i >= 4:
                        dve.wait_ge(sem("gate_spread"), i - 3)
                    nc.vector.tensor_scalar(diag[:, i % 4, :], eye, mod[:, l, 2 * CH + c, w:w + 1], None, ALU.mult)\
                      .then_inc(sem("gate_diag"), 1)

            def attention(st, gate, read_before):
                plan, lag = plans[st], LAG[st]
                ends, n = group_ends(st), len(plan)
                wait_used(dve, read_before)
                for i in range(n + lag + 4):
                    if i < n:
                        h, segs, _ = plan[i]
                        s = bank[S_BANK[i % 4]]
                        dve.wait_ge(*reached(st, "scores", i + 1))
                        if st == "s":
                            w = T5W
                            a = work[:, i % 2, 0:w]
                            dve.wait_ge(sem("s_log1p"), i + 1)
                            then(nc.vector.scalar_tensor_tensor(a, s[:, 0:w], 0.0, a, ALU.max, ALU.add), "s_full_softplus")
                            a3 = a.rearrange("p (b k) -> p b k", b=3)[:, ::2, :]
                            then(nc.vector.tensor_tensor(a3, a3, strict.unsqueeze(1).broadcast_to([P, 2, P]), ALU.mult),
                                 "s_past_softplus")
                            o = prob[:, i % 3, 0:w]
                            if i >= 3:
                                dve.wait_ge(*reached("s", "prob_turned", i - 2))
                            nc.vector.tensor_tensor_scan(o[:, P - 1::-1], ones[:, 0:P], a[:, P - 1::-1], 0.0, ALU.mult, ALU.add)
                            ins = nc.vector.tensor_tensor_scan(o[:, w - 1:P - 1:-1], ones[:, 0:TOK], a[:, w - 1:P - 1:-1], 0.0,
                                                               ALU.mult, ALU.add)
                            ins.then_inc(sem("s_softplus"), 1)
                            dve.wait_ge(sem("s_softplus"), i + 1)
                            then(nc.vector.tensor_tensor(o, s[:, 0:w], o, ALU.subtract), "s_unmasked")
                            o3 = o.rearrange("p (b k) -> p b k", b=3)[:, ::2, :]
                            nc.vector.tensor_tensor(o3, o3, negstrict.unsqueeze(1).broadcast_to([P, 2, P]), ALU.add)\
                              .then_inc(sem("s_log_weight"), 1)
                        else:
                            if st == "b":
                                dve.wait_ge(sem("b_bias_ready"), h + 1)
                                ins = nc.vector.tensor_tensor(s[:, 0:TOK], s[:, 0:TOK], bias_r[:, h % 2, segs[0][0], :], ALU.add)
                                ins.then_inc(sem("b_bias_used"), 1)
                                dve.wait_ge(sem("b_bias_used"), i + 1)
                            if st == "m":
                                dve.wait_ge(sem("m_bias_ready"), h + 1)
                                ins = nc.vector.tensor_tensor(s[:, 0:T5W], s[:, 0:T5W], bias_t[:, h % 2, :], ALU.add)
                                ins.then_inc(sem("m_bias_used"), 1)
                                dve.wait_ge(sem("m_bias_used"), i + 1)
                            if i >= 4:
                                dve.wait_ge(*reached(st, "exp", i - 3))
                            for j, (t, q0, k0, nk, c0) in enumerate(segs):
                                last = nc.vector.tensor_reduce(negmax[:, i % 4, j:j + 1], s[:, c0:c0 + nk], AX.X, ALU.max, negate=True)
                            last.then_inc(stage_sem["negmax"], 1)
                    u = i - 1
                    if st != "s" and 0 <= u < n:
                        segs = plan[u][1]
                        dve.wait_ge(*reached(st, "exp", u + 1))
                        then(nc.vector.reciprocal(inv[:, u % 4, 0:len(segs)], total[:, u % 4, 0:len(segs)]), "inv")
                        for j, (t, q0, k0, nk, c0) in enumerate(segs):
                            pr = prob[:, u % 3, c0:c0 + nk]
                            last = nc.vector.tensor_scalar(pr, pr, inv[:, u % 4, j:j + 1], None, ALU.mult)
                        last.then_inc(stage_sem["prob"], 1)
                    u = i - lag - 2
                    if u in ends:
                        p = ends[u]
                        dve.wait_ge(*reached(st, "mixed", u + 1))
                        if p >= 2:
                            dve.wait_ge(*reached(st, "out_hi", p - 1))
                            dve.wait_ge(*reached(st, "out_lo", p - 1))
                        b = bank[O_BANK[p % 2]]
                        o = work[:, 2 + p % 2, 0:TOK]
                        if gate:
                            ins = gate(p, b, o)
                        else:
                            ins = nc.vector.tensor_copy(o, b[:, 0:TOK])
                        ins.then_inc(stage_sem["gated"], 1)
                    u = i - lag - 3
                    if u in ends:
                        p = ends[u]
                        dst = h_lo[:, p % PAIRS, p // PAIRS * TOK:(p // PAIRS + 1) * TOK]
                        hi = h_hi[:, p % PAIRS, p // PAIRS * TOK:(p // PAIRS + 1) * TOK]
                        dve.wait_ge(*reached(st, "out_hi", p + 1))
                        dve.wait_ge(*reached(st, "gated", p + 1))
                        nc.vector.tensor_tensor(dst, work[:, 2 + p % 2, 0:TOK], hi.bitcast(F32), ALU.subtract)\
                          .then_inc(stage_sem["out_lo"], 1)

            def residual(name, st, tiles, gates):
                g0 = group_at[name]
                for cb in range(2):
                    split(at[name] + 2 * cb + 4)
                    cols = slice(cb * 512, (cb + 1) * 512)
                    for t in range(tiles):
                        g = g0 + cb * tiles + t
                        dve.wait_ge(product, g + 1)
                        x = xs[:, t, cols]
                        if gates:
                            tmp = work[:, g % 2, :]
                            if g - g0 >= 2:
                                dve.wait_ge(sem(st + "_x_done"), g - g0 - 1)
                            ins = nc.vector.tensor_tensor(tmp, bank[g % 4][:], gate_b[:, gates(t), cols], ALU.mult)
                            ins.then_inc(emptied["dve"], 1)
                            dve.wait_ge(emptied["dve"], emptied_by(g)[1])
                            ins = nc.vector.tensor_tensor(x, x, tmp, ALU.add)
                        else:
                            ins = nc.vector.tensor_tensor(x, x, bank[g % 4][:], ALU.add)
                            ins.then_inc(emptied["dve"], 1)
                            continue
                        ins.then_inc(sem(st + "_x_done"), 1)

            norm("n0", 4, lambda c, w: gain[:, 0, c, w:w + 1], lambda c, w: mod[:, 0, c, w:w + 1], None)
            split(at["a_in"] + 2)
            for cb in range(5):
                split(at["a_in"] + 2 * cb + 4)
                if cb >= 3:
                    continue
                heads = 8 if cb < 2 else 4
                w = heads * HD
                for tt in range(4):
                    j = 4 * cb + tt
                    sq, qn = prob_t[:, 0, 0:w], work[:, 0, 0:w]
                    src = prob[:, j % 3, 0:w]
                    dst = work[:, 2 + j % 2, :]
                    dve.wait_ge(emptied["act"], group_at["a_in"] + j + 1)
                    if j:
                        dve.wait_ge(sem("a_qk_done"), j)
                    then(nc.vector.tensor_tensor(sq, src, src, ALU.mult), "a_qk_square")
                    ss, v, r = stat[:, 0:heads], stat[:, 8:8 + heads], qk_root[:, 0:heads]
                    per_head = lambda ap: ap.rearrange("p (h d) -> p h d", d=HD)
                    then(nc.vector.tensor_reduce(ss, per_head(sq), AX.X, ALU.add), "a_qk_sum")
                    nc.vector.tensor_scalar(v, ss, 1.0 / HD, EPS, ALU.mult, ALU.add).then_inc(sem("a_qk_mean"), 1)
                    dve.wait_ge(sem("a_qk_root"), j + 1)
                    ins = nc.vector.tensor_tensor(per_head(qn), per_head(src), r.unsqueeze(2).broadcast_to([P, heads, HD]), ALU.mult)
                    ins.then_inc(sem("a_qk_normed"), 1)
                    dve.wait_ge(sem("a_qk_normed"), j + 1)
                    if j >= 2:
                        dve.wait_ge(sem("a_qk_turned"), j - 1)
                    outs = [per_head(dst)] if cb < 2 else [dst.rearrange("p (h u d) -> p h u d", u=2, d=HD)[:, :, u, :] for u in range(2)]
                    kind = 0 if cb < 2 else 1
                    if tt < TT:
                        dve.wait_ge(sem("rope_ready"), 1)
                        t1, t2 = prob_t[:, 0, 0:w], work[:, 1, 0:w]
                        by_head = lambda ap: ap.unsqueeze(1).broadcast_to([P, heads, HD])
                        nc.vector.tensor_tensor(per_head(t1), per_head(qn), by_head(rope[:, 2 * kind, tt, :]), ALU.mult)
                        five = lambda ap: ap.rearrange("p (h i) -> p h i", i=16)
                        sgn = rope[:, 2 * kind + 1, tt, :].rearrange("p (a b i) -> p a b i", a=2, b=2)
                        q5 = qn.rearrange("p (h a b i) -> p h a b i", a=2, b=2, i=16)
                        o5 = t2.rearrange("p (h a b i) -> p h a b i", a=2, b=2, i=16)
                        for a in range(2):
                            for half in range(2):
                                ins = nc.vector.tensor_tensor(o5[:, :, a, half, :], q5[:, :, a, 1 - half, :],
                                                              sgn[:, a, half, :].unsqueeze(1).broadcast_to([P, heads, 16]), ALU.mult)
                        then(ins, "a_qk_rotated")
                        for o in outs:
                            ins = nc.vector.tensor_tensor(o, per_head(t1), per_head(t2), ALU.add)
                    else:
                        for o in outs:
                            ins = nc.vector.tensor_tensor(o, per_head(qn), qk_g[:, kind, :].unsqueeze(1).broadcast_to([P, heads, HD]), ALU.mult)
                    ins.then_inc(sem("a_qk_done"), 1)

            def gate_a(p, b, o):
                w = p // PAIRS
                return nc.vector.tensor_tensor(o, b[:, 0:TOK], z_a[:, p % PAIRS, w * TOK:(w + 1) * TOK], ALU.mult)

            gate_rows(0, 0, 0)
            gate_rows(0, 1, 1)
            dve.wait_ge(emptied["act"], group_at["a_out"])
            attention("a", gate_a, last_unit["a_in"])
            dve.wait_ge(sem("gate_copied"), 4)
            residual("a_out", "a", 4, lambda t: t // TT)
            if done("a"):
                return

            norm("n1", 4, lambda c, w: gain[:, 1, c, w:w + 1], lambda c, w: mod[:, 1, c, w:w + 1], last_unit["a_out"])
            for cb in range(8):
                split(at["b_in"] + 2 * cb + 4)
            gate_rows(1, 0, 2)

            def gate_bx(p, b, o):
                unflip = lambda ap: ap.rearrange("p (t n) -> p t n", t=TT)
                return nc.vector.tensor_tensor(unflip(o), unflip(b[:, 0:TOK])[:, :, ::-1], unflip(z_b[:, p, :]), ALU.mult)

            dve.wait_ge(emptied["act"], emptied_by(group_at["b_in"] + 31)[1])
            attention("b", gate_bx, last_unit["b_in"])
            dve.wait_ge(sem("gate_copied"), 6)
            residual("b_out", "b", 2, lambda t: 0)
            if done("b"):
                return
            r = roots("f1", TT)
            dve.wait_ge(sem("final_gain_landed"), 16)
            for t in range(TT):
                nc.vector.scalar_tensor_tensor(xs[:, t, :], xs[:, t, :], r[:, t:t + 1], gate_b[:, 1, :], ALU.mult, ALU.mult)\
                  .then_inc(sem("f1_x_done"), 1)
            dve.wait_ge(sem("f1_x_done"), 2)

            norm("n2", 2, lambda c, w: vec_t[:, V_MIX + c:V_MIX + c + 1], None, last_unit["b_out"])
            for cb in range(6):
                split(at["qkv0"] + 2 * cb + 4)
            attention("s", None, last_unit["qkv0"])
            residual("o0", "o0", 2, None)
            norm("n3", 2, lambda c, w: vec_t[:, V_FFN + c:V_FFN + c + 1], None, last_unit["o0"])
            g0 = group_at["ff"]
            for j in range(HF):
                split(ff_at[1, j] + 3)
                split(ff_at[3, j] + 3)
                dve.wait_ge(product, g0 + 2 * j + 2)
                dve.wait_ge(emptied["act"], emptied_by(g0 + 2 * j)[1])
                if j >= 2:
                    dve.wait_ge(sem("ff_hid_hi"), j - 1)
                    dve.wait_ge(sem("ff_hid_lo"), j - 1)
                nc.vector.tensor_tensor(hid_f[:, j % 2, :], hid_s[:, j % 2, :], bank[(g0 + 2 * j + 1) % 4][:], ALU.mult)\
                  .then_inc(emptied["dve"], 1)
                dve.wait_ge(emptied["dve"], emptied_by(g0 + 2 * j + 1)[1])
                dve.wait_ge(sem("ff_hid_hi"), j + 1)
                if j >= 2:
                    wait_used(dve, ff_at[2, j - 2])
                nc.vector.tensor_tensor(hid_lo[:, j % 2, :], hid_f[:, j % 2, :], hid_hi[:, j % 2, :].bitcast(F32), ALU.subtract)\
                  .then_inc(sem("ff_hid_lo"), 1)
                split(ff_at[1, min(j + 1, HF - 1)] + 2)
            split(at["qkv1"] + 2)
            wait_used(dve, last_unit["ff"])
            for t in range(TT):
                for half in range(2):
                    x = xs[:, t, half * 512:(half + 1) * 512]
                    nc.vector.tensor_tensor(x, x, bank[4 + 2 * t + half][:], ALU.add).then_inc(sem("ff_x_done"), 1)
            dve.wait_ge(sem("ff_x_done"), 4)
            norm("n4", 2, lambda c, w: vec_t[:, V_MIX + CH + c:V_MIX + CH + c + 1], None, last_unit["ff"])
            for cb in range(6):
                split(at["qkv1"] + 2 * cb + 4)

            def unflip_copy(p, b, o):
                unflip = lambda ap: ap.rearrange("p (t n) -> p t n", t=TT)
                return nc.vector.tensor_copy(unflip(o), unflip(b[:, 0:TOK])[:, :, ::-1])

            split(NS - 1)
            attention("m", unflip_copy, last_unit["qkv1"])
            split(NS)
            dve.wait_ge(lo_ready, NS)
            for i in range(3):
                dve.nop().then_inc(x_raw_free, 1)
            residual("o1", "o1", 2, None)
            if done("f"):
                return
            dve.wait_ge(*x_done_in("o1"))
            for i in range(3):
                dve.nop().then_inc(x_raw_free, 1)
            for i in range(4):
                dve.nop().then_inc(sem("x_added"), 1)

            chain = [0]

            def link(ins):
                chain[0] += 1
                ins.then_inc(sem("routing_step"), 1)
                dve.wait_ge(sem("routing_step"), chain[0])

            r = roots("n5", TT)
            dve.wait_ge(sem("ffn_gain_landed"), 16)
            for t in range(TT):
                nc.vector.scalar_tensor_tensor(xs[:, TT + t, :], xs[:, t, :], r[:, t:t + 1], gate_b[:, 0, :], ALU.mult, ALU.mult)\
                  .then_inc(sem("n5_h_ready"), 1)
            link(nc.vector.memset(visits[:], 0.0))
            link(nc.vector.memset(ids_f[:], 0.0))
            dve.wait_ge(sem("route_landed"), 32)
            count = route[:, P:P + EXP]
            for t in range(TT):
                dve.wait_ge(sem("logits"), t + 1)
                link(nc.vector.tensor_copy(logit[:, t, :], bank[3 * (1 - t)][:, 0:EXP]))
                link(nc.vector.max(best[:, t, :], logit[:, t, :]))
                link(nc.vector.max_index(best_i[:, t, :], best[:, t, :], logit[:, t, :]))
            link(nc.vector.tensor_copy(best_f[:], best_i[:, :, 0:2]))
            nc.vector.tensor_tensor(gates[:, :, 0], best[:, :, 1], best[:, :, 0], ALU.subtract).then_inc(sem("gap_ready"), 1)
            for t in range(TT):
                for i in range(2):
                    link(nc.vector.tensor_scalar(hot[:, t, i, :], count, best_f[:, t, i:i + 1], None, ALU.is_equal))
                nc.vector.tensor_tensor(facts[:, 2 + t, :], hot[:, t, 0, :], hot[:, t, 1, :], ALU.add).then_inc(sem("chosen"), 1)
            dve.wait_ge(sem("gap_exp"), 1)
            link(nc.vector.tensor_scalar(gates[:, :, 2], gates[:, :, 1], 1.0, None, ALU.add))
            link(nc.vector.reciprocal(gates[:, :, 2], gates[:, :, 2]))
            link(nc.vector.tensor_tensor(gates[:, :, 3], gates[:, :, 1], gates[:, :, 2], ALU.mult))
            for t in range(TT):
                link(nc.vector.tensor_scalar(facts[:, 4 + t, :], hot[:, t, 0, :], gates[:, t, 2:3], None, ALU.mult))
                link(nc.vector.scalar_tensor_tensor(facts[:, 4 + t, :], hot[:, t, 1, :], gates[:, t, 3:4], facts[:, 4 + t, :], ALU.mult, ALU.add))
            dve.wait_ge(sem("slots"), 3)
            for t in range(TT):
                link(nc.vector.tensor_copy(facts[:, t, :], bank[1 + t][:, 0:EXP]))
            link(nc.vector.tensor_copy(over[:, 0, :], bank[4][:, 0:EXP]))
            link(nc.vector.tensor_copy(visits[:, 0:EXP, :], facts[:].rearrange("p q e -> p e q")))
            link(nc.vector.tensor_scalar(over[:, 1, :], over[:, 0, :], float(P), None, ALU.is_gt))
            link(nc.vector.tensor_tensor_scan(over[:, 2, :], ones[:, 0:EXP], over[:, 1, :], 0.0, ALU.mult, ALU.add))
            link(nc.vector.tensor_tensor(over[:, 3, :], over[:, 2, :], over[:, 1, :], ALU.subtract))
            for i in range(MAXOVER):
                link(nc.vector.scalar_tensor_tensor(over_hot[:, i, :], over[:, 3, :], float(i), over[:, 1, :], ALU.is_equal, ALU.mult))
                for q in range(6):
                    ins = nc.vector.tensor_tensor(over_tmp[:, i, q, :], over_hot[:, i, :], facts[:, q, :], ALU.mult)
                link(ins)
            link(nc.vector.tensor_reduce(visits[:, EXP:EXP + MAXOVER, :], over_tmp[:], AX.X, ALU.add))
            link(nc.vector.tensor_scalar(visits[:, EXP:EXP + MAXOVER, 0:TT], visits[:, EXP:EXP + MAXOVER, 0:TT], -float(P), None, ALU.add))
            for i in range(MAXOVER):
                ins = nc.vector.tensor_tensor(over_tmp[:, i, 0, :], over_hot[:, i, :], count, ALU.mult)
            link(ins)
            link(nc.vector.tensor_copy(ids_f[:, 0:EXP], count))
            link(nc.vector.tensor_reduce(ids_f[:, EXP:EXP + MAXOVER], over_tmp[:, :, 0, :], AX.X, ALU.add))
            link(nc.vector.tensor_scalar(ids_f[:, 12:13], over[:, 2, EXP - 1:EXP], float(EXP), None, ALU.add))
            nc.vector.tensor_copy(ids[:], ids_f[:]).then_inc(sem("routed"), 1)

            def picks(v):
                nc.vector.tensor_scalar(current[:], visits[:, bass.ds(v, 1), :].rearrange("p a q -> p (a q)"), 0.0, None, ALU.add)\
                  .then_inc(sem("current_ready"), 1)
                dve.wait_ge(sem("current_ready"), v + 1)
                for t in range(TT):
                    ins = nc.vector.tensor_scalar(pick[:, t, :], route[:, P:2 * P], current[:, t:t + 1], current[:, 2 + t:3 + t],
                                                  ALU.is_equal, ALU.mult)
                ins.then_inc(sem("pick_ready"), 1)
                dve.wait_ge(sem("pick_ready"), v + 1)
                for t in range(TT):
                    ins = nc.vector.tensor_scalar(pick_g[:, t, :], pick[:, t, :], current[:, 4 + t:5 + t], None, ALU.mult)
                ins.then_inc(sem("pick_g_ready"), 1)

            def gathered(n):
                for b in range(2):
                    dve.wait_ge(sem("xe_hi_ready"), 2 * n + b - 1)
                    cols = slice(4 * b, 4 * b + 4)
                    nc.vector.tensor_tensor(xe_lo[:, cols, :].rearrange("p c s -> p (c s)"), bank[6 + b][:],
                                            xe_hi[:, cols, :].rearrange("p c s -> p (c s)").bitcast(F32), ALU.subtract)\
                      .then_inc(sem("xe_lo_ready"), 1)

            picks(0)
            gathered(1)
            dve.wait_ge(sem("routed"), 1)
            n_visits = dve.value_load(ids[0:1, 12:13], min_val=EXP, max_val=EXP + MAXOVER)
            with dve.Fori(0, n_visits) as v:
                def rest_unit(k):
                    dve.wait_ge(x_hi_ready, v * NV + k + 1)
                    nc.vector.tensor_tensor(ring6(w_lo, w_lo_x, k, 1)[:, 0, :], ring6(raw, raw_x, k, 1)[:, 0, :],
                                            ring6(w_hi, w_hi_x, k, 1)[:, 0, :].bitcast(F32), ALU.subtract).then_inc(x_raw_free, 1)

                def turned(j):
                    dve.wait_ge(sem("act_hi_ready"), v * NJ + j + 1)
                    nc.vector.tensor_tensor(act_lo[:], bank[2][:], act_hi[:].bitcast(F32), ALU.subtract).then_inc(sem("act_lo_ready"), 1)

                for k in range(6):
                    rest_unit(k)
                for k, (kind, j, half) in enumerate(visit_units):
                    if half:
                        if kind == 1 and j:
                            turned(j - 1)
                        if kind == 3:
                            dve.wait_ge(x_split_free, v * NV + k + 7)
                            dve.wait_ge(sem("act_s_ready"), v * NJ + j + 1)
                            nc.vector.tensor_tensor(act_f[:], act_s[:], bank[1][:], ALU.mult).then_inc(sem("act_f_ready"), 1)
                            if j == 3:
                                dve.wait_ge(sem("pick_turned"), v + 1)
                                picks(v + 1)
                        if kind == 2 and j == NJ - 2:
                            gathered(v + 2)
                            turned(NJ - 1)
                        if kind == 2 and j == NJ - 1:
                            for i in range(4):
                                dve.wait_ge(sem("x_combined"), v * 4 + i + 1)
                                x = xs[:, i // 2, i % 2 * 512:(i % 2 + 1) * 512]
                                nc.vector.tensor_tensor(x, x, bank[(3, 6, 7, 2)[i]][:], ALU.add).then_inc(sem("x_added"), 1)
                    if k + 6 < NV:
                        rest_unit(k + 6)

            r = roots("n6", TT)
            dve.wait_ge(sem("last_gain_landed"), 16)
            for t in range(TT):
                nc.vector.scalar_tensor_tensor(xs[:, TT + t, :], xs[:, t, :], r[:, t:t + 1], gate_b[:, 1, :], ALU.mult, ALU.mult)\
                  .then_inc(sem("y_done"), 1)

        @block.gpsimd
        def _(pool):
            def root(st, tiles):
                pool.wait_ge(*reached(st, "mean", 1))
                nc.gpsimd.tensor_tensor(stat[:, 8:8 + tiles], stat[:, 4:4 + tiles], minus_half[:, 0:tiles], ALU.pow)\
                  .then_inc(stage_sem["root"], 1)

            pool.wait_ge(sem("ones_ready"), 2)
            root("n0", 4)
            for j in range(12):
                heads = 8 if j < 8 else 4
                pool.wait_ge(sem("a_qk_mean"), j + 1)
                nc.gpsimd.tensor_tensor(qk_root[:, 0:heads], stat[:, 8:8 + heads], minus_half[:, 0:heads], ALU.pow)\
                  .then_inc(sem("a_qk_root"), 1)
            if done("a"):
                return
            root("n1", 4)
            pool.wait_ge(sem("constants_landed"), 32)
            for h in range(HEADS):
                pool.wait_ge(sem(f"near_bias_landed_{h % 2}"), 64 * (h // 2 + 1))
                b = bias_r[:, h % 2, :, :].rearrange("p t (r c) -> p (t r) c", c=GRID_W)
                nc.gpsimd.tensor_tensor(b, b, near.unsqueeze(1).broadcast_to([P, TT * GROWS, GRID_W]), ALU.add)\
                  .then_inc(sem("b_bias_ready"), 1)
            if done("b"):
                return
            pool.wait_ge(sem("a_x_done"), 8)
            pool.dma_start(gate_b[:, 1, :], bass.AP(A["final_norm_g"].tensor, 0, [[0, P], [1, D]]))\
                .then_inc(sem("final_gain_landed"), 16)
            root("f1", TT)
            root("n2", TT)
            root("n3", TT)
            root("n4", TT)
            for h in range(HEADS):
                pool.wait_ge(sem(f"t5_bias_landed_{h % 2}"), 32 * (h // 2 + 1))
                nc.gpsimd.tensor_tensor(bias_t[:, h % 2, :], bias_t[:, h % 2, :], causal, ALU.add)\
                  .then_inc(sem("m_bias_ready"), 1)
            if done("f"):
                return
            pool.wait_ge(sem("f1_x_done"), 2)
            pool.dma_start(gate_b[:, 0, :], bass.AP(A["ffn_norm_2"].tensor, D, [[0, P], [1, D]])).then_inc(sem("ffn_gain_landed"), 16)
            pool.dma_start(gate_b[:, 1, :], bass.AP(A["final_norm_2"].tensor, 0, [[0, P], [1, D]])).then_inc(sem("last_gain_landed"), 16)
            pool.dma_start(route[:], A["route"]).then_inc(sem("route_landed"), 16)
            pool.dma_start(router_w[:], router.rearrange("(c p) e -> p c e", p=P)).then_inc(sem("route_landed"), 16)
            root("n5", TT)
            root("n6", TT)

        @block.tensor
        def _(pe):
            def three(out_, a_hi, a_lo, b_hi, b_lo, start, stop):
                nc.tensor.matmul(out_, a_hi, b_hi, start=start, stop=False)
                nc.tensor.matmul(out_, a_hi, b_lo, start=False, stop=False)
                return nc.tensor.matmul(out_, a_lo, b_hi, start=False, stop=stop)

            pe.wait_ge(sem("vectors_landed"), 96)
            pe.wait_ge(sem("constants_landed"), 32)
            nc.tensor.transpose(bank[6][:, 0:NVEC], work[0:NVEC, 0, 0:P], eye[0:NVEC, 0:NVEC]).then_inc(sem("vec_turned"), 1)
            pe.wait_ge(sem("t5_landed"), 32)
            nc.tensor.matmul(bank[7][0:HEADS, 0:T5W], work[0:BUCKETS, 3, 0:HEADS], work[0:BUCKETS, 2, 0:T5W],
                             start=True, stop=True).then_inc(sem("t5_rows"), 1)

            pe.wait_ge(sem("silu_c_ready"), 1)
            for n in range(NMOD):
                pe.wait_ge(landed[n % NRAW], 16 * (n // NRAW + 1))
                w = unit_view(raw, n, 4)
                cb, half = n // 2, n % 2
                if half == 0 and cb >= 2:
                    pe.wait_ge(sem("mod_ready"), cb - 1)
                if n == 2:
                    pe.wait_ge(sem("t5_copied"), 1)
                for i in range(4):
                    for c in range(4):
                        last = nc.tensor.matmul(bank[4 * (cb % 2) + i][:, 0:2], w[:, c, i * P:(i + 1) * P],
                                                silu_c[:, 4 * half + c, :], start=(half == 0 and c == 0),
                                                stop=(half == 1 and c == 3))
                last.then_inc(mod_used, 1)

            def norm(st, tiles):
                pe.wait_ge(*reached(st, "diag", tiles))
                for c in range(CH):
                    if c >= 4:
                        pe.wait_ge(*reached(st, "h_lo", c - 3))
                    for t in range(tiles):
                        last = nc.tensor.matmul(bank[4 + c % 4][:, t * P:(t + 1) * P], xs[:, t, c * P:(c + 1) * P], diag[:, t, :],
                                                start=True, stop=True)
                    last.then_inc(stage_sem["transposed"], 1)
                pe.wait_ge(*reached(st, "h_lo", CH))

            def linear(name, blocks, forms, after=None):
                g = group_at[name]
                for cb in range(blocks):
                    form = forms(cb)
                    for half in range(2):
                        m = at[name] + 2 * cb + half
                        pe.wait_ge(lo_ready, m + 1)
                        hi, lo = unit_view(w_hi, m, 4), unit_view(w_lo, m, 4)
                        for i, f in enumerate(form):
                            if half == 0 and g + i >= 4:
                                who, n = emptied_by(g + i - 4)
                                pe.wait_ge(emptied[who], n)
                            b = bank[(g + i) % 4]
                            for c in range(4):
                                k = 4 * half + c
                                first_, last_ = half == 0 and c == 0, half == 1 and c == 3
                                if f[0] == "rows":
                                    cols = slice(f[1] * P, (f[1] + 1) * P)
                                    ins = three(b[:], h_hi[:, k, cols], h_lo[:, k, cols], hi[:, c, :], lo[:, c, :], first_, last_)
                                else:
                                    cols = slice(f[1] * P, (f[1] + 1) * P)
                                    ins = three(b[:, 0:f[2]], hi[:, c, cols], lo[:, c, cols], h_hi[:, k, 0:f[2]], h_lo[:, k, 0:f[2]],
                                                first_, last_)
                            if half:
                                ins.then_inc(product, 1)
                        if not half:
                            ins.then_inc(w_used, 1)
                    g += len(form)
                    if after:
                        after(cb)

            def attention(st):
                plan, lag = plans[st], LAG[st]
                starts, n = group_starts(st), len(plan)
                for i in range(n + lag + 1):
                    if i < n:
                        h, segs, _ = plan[i]
                        par = h % 2 * HD
                        if i >= 4:
                            if st == "s":
                                pe.wait_ge(sem("s_log_weight"), i - 3)
                            else:
                                pe.wait_ge(*reached(st, "exp", i - 3))
                        b = bank[S_BANK[i % 4]]
                        for t, q0, k0, nk, c0 in segs:
                            last = nc.tensor.matmul(b[:, c0:c0 + nk], query_operand(st, h, q0),
                                                    key_operand(st, h, k0, nk), start=True, stop=True)
                        last.then_inc(stage_sem["scores"], 1)
                    u = i - lag
                    if 0 <= u < n:
                        pe.wait_ge(*reached(st, "prob", u + 1))
                        if u >= 2:
                            pe.wait_ge(*reached(st, "prob_t", u - 1))
                        w = sum(x[3] for x in plan[u][1])
                        for k in range(w // P):
                            last = nc.tensor.transpose(bank[T_BANK[u % 2]][:, k * P:(k + 1) * P], prob[:, u % 3, k * P:(k + 1) * P], eye)
                        last.then_inc(stage_sem["prob_turned"], 1)
                    u = i - lag - 1
                    if 0 <= u < n:
                        h, segs, p = plan[u]
                        par = h % 2 * HD
                        if u in starts and p >= 2:
                            pe.wait_ge(*reached(st, "gated", p - 1))
                        pe.wait_ge(*reached(st, "prob_t", u + 1))
                        b = bank[O_BANK[p % 2]]
                        for t, q0, k0, nk, c0 in segs:
                            for k in range(nk // P):
                                last = nc.tensor.matmul(b[par:par + HD, t * P:(t + 1) * P], value_operand(st, h, k0 // P + k),
                                                        prob_t[:, u % 2, c0 + k * P:c0 + (k + 1) * P],
                                                        start=(k == 0), stop=(k == nk // P - 1))
                        last.then_inc(stage_sem["mixed"], 1)
                pe.wait_ge(*reached(st, "out_lo", max(group_ends(st).values()) + 1))

            def gate_rows(k, halves0):
                for c in range(CH):
                    i = k * CH + c
                    pe.wait_ge(sem("gate_diag"), i + 1)
                    hv = halves0 + c // 4
                    if c % 4 == 0 and hv >= 4:
                        pe.wait_ge(sem("gate_copied"), hv - 3)
                    ins = nc.tensor.matmul(bank[4 + hv % 4][:, c % 4 * P:(c % 4 + 1) * P], ones[:, 0:P], diag[:, i % 4, :], start=True, stop=True)
                    ins.then_inc(sem("gate_spread"), 1)

            rows = lambda n: [("rows", t) for t in range(n)]
            cols = lambda n: [("cols", i, n) for i in range(4)]

            norm("n0", 4)

            def turn_a(cb):
                if not 1 <= cb <= 3:
                    return
                for tt in range(4):
                    j = 4 * (cb - 1) + tt
                    pe.wait_ge(sem("a_qk_done"), j + 1)
                    if j >= 4:
                        pe.wait_ge(sem("a_qk_kept"), j - 3)
                    for k in range(4):
                        last = nc.tensor.transpose(bank[4 + j % 4][:, k * P:(k + 1) * P], work[:, 2 + j % 2, k * P:(k + 1) * P], eye)
                    last.then_inc(sem("a_qk_turned"), 1)

            linear("a_in", 5, lambda cb: rows(4) if cb < 3 else cols(2 * TOK), turn_a)
            pe.wait_ge(sem("a_qk_kept"), 12)
            gate_rows(0, 0)
            gate_rows(1, 2)
            pe.wait_ge(sem("gate_copied"), 4)
            pe.wait_ge(emptied["act"], group_at["a_out"])
            attention("a")
            linear("a_out", 2, lambda cb: rows(4))
            if done("a"):
                return

            norm("n1", 4)
            linear("b_in", 8, lambda cb: cols(TOK) if cb < 2 or cb >= 6 else cols(2 * TOK) if cb < 4 else rows(4))
            gate_rows(2, 4)
            pe.wait_ge(sem("gate_copied"), 6)
            pe.wait_ge(emptied["act"], emptied_by(group_at["b_in"] + 31)[1])
            attention("b")
            linear("b_out", 2, lambda cb: rows(2))
            if done("b"):
                return

            norm("n2", 2)
            linear("qkv0", 6, lambda cb: cols(TOK) if cb < 4 else rows(2))
            pe.wait_ge(emptied["act"], emptied_by(group_at["qkv0"] + 19)[1])
            attention("s")
            linear("o0", 2, lambda cb: rows(2))
            norm("n3", 2)
            g0 = group_at["ff"]

            def ff_out(j):
                m = ff_at[2, j]
                pe.wait_ge(lo_ready, m + 1)
                pe.wait_ge(sem("ff_hid_lo"), j + 1)
                hi, lo = unit_view(w_hi, m, 2), unit_view(w_lo, m, 2)
                for t in range(TT):
                    for half in range(2):
                        for c in range(2):
                            tok = slice(c * TOK + t * P, c * TOK + (t + 1) * P)
                            n = slice(half * 512, (half + 1) * 512)
                            ins = three(bank[4 + 2 * t + half][:], hid_hi[:, j % 2, tok], hid_lo[:, j % 2, tok], hi[:, c, n], lo[:, c, n],
                                        j == 0 and c == 0, j == HF - 1 and c == 1)
                ins.then_inc(w_used, 1)

            for j in range(HF):
                for kind in (1, 3):
                    m = ff_at[kind, j]
                    g = g0 + 2 * j + (kind == 3)
                    pe.wait_ge(lo_ready, m + 1)
                    who, n = emptied_by(g - 4)
                    pe.wait_ge(emptied[who], n)
                    hi, lo = unit_view(w_hi, m, 8), unit_view(w_lo, m, 8)
                    for i in range(2):
                        for c in range(CH):
                            f = slice(i * P, (i + 1) * P)
                            ins = three(bank[g % 4][:, i * TOK:(i + 1) * TOK], hi[:, c, f], lo[:, c, f], h_hi[:, c, 0:TOK], h_lo[:, c, 0:TOK],
                                        c == 0, c == CH - 1)
                    ins.then_inc(product, 1)
                if j:
                    ff_out(j - 1)
            ff_out(HF - 1)
            norm("n4", 2)
            linear("qkv1", 6, lambda cb: cols(TOK) if cb < 4 else rows(2))
            pe.wait_ge(emptied["act"], emptied_by(group_at["qkv1"] + 19)[1])
            attention("m")
            linear("o1", 2, lambda cb: rows(2))
            if done("f"):
                return

            pe.wait_ge(product, len(group_engine))
            pe.wait_ge(*x_done_in("o1"))
            for i in range(6):
                pe.nop().then_inc(x_split_free, 1)
            pe.wait_ge(sem("route_landed"), 32)
            pe.wait_ge(sem("n5_h_ready"), TT)
            for t in range(TT):
                if t:
                    pe.wait_ge(sem("logits"), t)
                for half in range(2):
                    if t:
                        pe.wait_ge(sem("n5_turned_kept"), half + 1)
                    for c in range(4):
                        k = 4 * half + c
                        ins = nc.tensor.transpose(bank[6 + half][:, c * P:(c + 1) * P], xs[:, TT + t, k * P:(k + 1) * P], eye)
                    ins.then_inc(sem("n5_turned"), 1)
                pe.wait_ge(sem("n5_turned_kept"), 2 * t + 2)
                for c in range(CH):
                    ins = nc.tensor.matmul(bank[3 * (1 - t)][:, 0:EXP], y_e[:, c * P:(c + 1) * P], router_w[:, c, :],
                                           start=(c == 0), stop=(c == CH - 1))
                ins.then_inc(sem("logits"), 1)
            pe.wait_ge(sem("chosen"), 2)
            before, every = route[:, 0:P], ones[:, 0:P]
            nc.tensor.matmul(bank[1][:, 0:EXP], before, facts[:, 2, :], start=True, stop=True).then_inc(sem("slots"), 1)
            nc.tensor.matmul(bank[2][:, 0:EXP], before, facts[:, 3, :], start=True, stop=False)
            nc.tensor.matmul(bank[2][:, 0:EXP], every, facts[:, 2, :], start=False, stop=True).then_inc(sem("slots"), 1)
            nc.tensor.matmul(bank[4][:, 0:EXP], every, facts[:, 2, :], start=True, stop=False)
            nc.tensor.matmul(bank[4][:, 0:EXP], every, facts[:, 3, :], start=False, stop=True).then_inc(sem("slots"), 1)

            def gather(v):
                pe.wait_ge(sem("pick_ready"), v + 1)
                for b in range(2):
                    for c in range(4):
                        for t in range(TT):
                            k = 4 * b + c
                            ins = nc.tensor.matmul(bank[6 + b][:, c * P:(c + 1) * P], xs[:, TT + t, k * P:(k + 1) * P], pick[:, t, :],
                                                   start=(t == 0), stop=(t == TT - 1))
                    ins.then_inc(sem("x_gathered"), 1)

            gather(0)
            pe.wait_ge(sem("routed"), 1)
            n_visits = pe.value_load(ids[0:1, 12:13], min_val=EXP, max_val=EXP + MAXOVER)
            with pe.Fori(0, n_visits) as v:
                def turn(j):
                    pe.wait_ge(sem("act_f_ready"), v * NJ + j + 1)
                    for c in range(4):
                        ins = nc.tensor.transpose(bank[2][:, c * P:(c + 1) * P], act_f[:, c * P:(c + 1) * P], eye)
                    ins.then_inc(sem("x_turned"), 1)

                pe.wait_ge(sem("xe_lo_ready"), v * 2 + 2)
                for k, (kind, j, half) in enumerate(visit_units):
                    if kind == 1 and half == 0 and j:
                        pe.wait_ge(sem("act_s_ready"), v * NJ + j)
                    if kind == 3 and half == 0 and j:
                        if j == 1:
                            pe.wait_ge(sem("x_added"), v * 4 + 4)
                        turn(j - 1)
                        if j == 2:
                            pe.wait_ge(sem("pick_g_ready"), v + 1)
                            for t in range(TT):
                                ins = nc.tensor.transpose(bank[3][:, t * P:(t + 1) * P], pick_g[:, t, :], eye)
                            ins.then_inc(sem("pick_turned"), 1)
                    if kind == 2 and half == 0:
                        if j == NJ - 1:
                            gather(v + 1)
                            turn(j)
                        pe.wait_ge(sem("act_lo_ready"), v * NJ + j + 1)
                    pe.wait_ge(x_raw_free, v * NV + k + 7)
                    hi, lo = ring6(w_hi, w_hi_x, k, 4), ring6(w_lo, w_lo_x, k, 4)
                    for c in range(4):
                        if kind == 2:
                            a = slice(c * P, (c + 1) * P)
                            ins = three(bank[4 + half][:], act_hi[:, a], act_lo[:, a], hi[:, c, :], lo[:, c, :],
                                        j == 0 and c == 0, j == NJ - 1 and c == 3)
                        else:
                            ins = three(bank[kind // 2][:], xe_hi[:, 4 * half + c, :], xe_lo[:, 4 * half + c, :], hi[:, c, :], lo[:, c, :],
                                        half == 0 and c == 0, half == 1 and c == 3)
                    ins.then_inc(x_split_free, 1)
                pe.wait_ge(sem("pick_gt_ready"), v + 1)
                pe.wait_ge(sem("xe_lo_ready"), v * 2 + 4)
                for i in range(4):
                    t, half = i // 2, i % 2
                    if i < 2:
                        pe.wait_ge(sem("y_ready"), v * 2 + half + 1)
                    nc.tensor.matmul(bank[(3, 6, 7, 2)[i]][:], pick_gt[:, t * P:(t + 1) * P], y_e[:, half * 512:(half + 1) * 512],
                                     start=True, stop=True).then_inc(sem("x_combined"), 1)


INPUTS = ["x", "c", "ctx", "c_ctx", "norm_g", "w_mod", "b_mod", "a_w_in", "a_q_norm_g", "a_k_norm_g", "a_w_out", "b_w_in",
          "b_rpb", "b_w_out", "final_norm_g", "w_qkv_2", "w_o_2", "mixer_norm_2", "ffn_norm_2", "rel_bias_2", "w1_2", "w3_2",
          "w2_2", "router_2", "e_w1_2", "e_w3_2", "e_w2_2", "final_norm_2"]

STOP = None


def kernel(**inputs):
    import concourse.bacc as bacc
    from concourse.bass_utils import run_bass_kernel_spmd
    nc = bacc.Bacc("TRN2", target_bir_lowering=False, num_devices=1)
    arrays = {name: np.ascontiguousarray(inputs[name]) for name in INPUTS}
    arrays.update(zip(("keep", "once", "onehot", "route"), shape_constants()))
    A = {k: nc.dram_tensor("in_" + k, a.shape, mybir.dt.from_np(a.dtype), kind="ExternalInput").ap() for k, a in arrays.items()}
    out = nc.dram_tensor("out_0", (1, TOK, D), F32, kind="ExternalOutput").ap()
    build(nc, A, out, stop=STOP)
    r = run_bass_kernel_spmd(nc, [{"in_" + k: a for k, a in arrays.items()}], core_ids=[0])
    return r.results[0]["out_0"]
```

```python
from contextlib import ExitStack

import numpy as np
import concourse.bass as bass
from concourse import mybir

ALU = mybir.AluOpType
ACT = mybir.ActivationFunctionType
AX = mybir.AxisListType
F32 = mybir.dt.float32
F32R = mybir.dt.float32r
I32 = mybir.dt.int32
U32 = mybir.dt.uint32

P = 128
D = 1024
CH = D // P
TOK = 256
TT = TOK // P
HEADS, HD = 16, 64
PAIRS = HEADS // 2
KVH = 4
GRID_W = 64
GROWS = TOK // GRID_W
RPB_R, RPB_C = 15, 31
BUCKETS = 32
FF = 2816
EXP, FE = 8, 3584
UW = 2048
NRAW, NSPLIT = 3, 3
NEG = -1e30
EPS = 1e-6
T5W = 384
HF = FF // 256
BIAS_RING = 8
MAXOVER = 3

V_NORM, V_BMOD, V_MIX, V_FFN, V_C = 0, 16, 64, 80, 96
NVEC = 112


def shape_constants():
    f = np.float32
    tok = np.arange(TOK)
    inv = f(10000.0) ** (-np.arange(0, 32, 2, dtype=f) / f(32))
    ang = np.stack([(tok // GRID_W).astype(f)[:, None] * inv, (tok % GRID_W).astype(f)[:, None] * inv], 1)
    cos, sin = np.cos(ang), np.sin(ang)
    cos64 = np.stack([cos, cos], 2).reshape(TT, P, HD)
    sin64 = np.stack([-sin, sin], 2).reshape(TT, P, HD)
    q, k = np.arange(P)[:, None], np.arange(P)[None, :]
    col = GRID_W - 1 - np.arange(P) % GRID_W
    c0 = np.clip(col - 8, 0, GRID_W - 16)[:, None]
    kc = np.arange(GRID_W)[None, :]
    near = np.where((kc >= c0) & (kc < c0 + 16), 0.0, NEG)
    strict = (k < q).astype(f)
    causal = np.concatenate([np.where(k <= P - 1 - q, 0.0, NEG),
                             np.where(np.arange(TOK)[None, :] <= TOK - 1 - q, 0.0, NEG)], 1)
    keep = np.concatenate([np.eye(P), near, strict, np.where(strict > 0, 0.0, NEG), causal], 1).astype(f)
    once = np.concatenate([cos64[0], cos64[1], sin64[0], sin64[1]], 1).astype(f)
    n = np.maximum(TOK - 1 - np.arange(T5W), 0)
    large = 16 + (np.log(np.maximum(n, 1).astype(f) / f(16)) / f(np.log(8.0)) * f(16)).astype(np.int32)
    bucket = np.where(n < 16, n, np.minimum(large, BUCKETS - 1))
    onehot = (bucket[None, :] == np.arange(BUCKETS)[:, None]).astype(f)
    route = np.concatenate([(q < k).astype(f), np.broadcast_to(k, (P, P)).astype(f)], 1)
    spread = np.stack([np.arange(2 * P) // P == r % 2 for r in range(4)]).astype(f)
    return keep, once, onehot, np.ascontiguousarray(route), spread


K_ID, K_NEAR, K_STRICT, K_NEGS, K_CAUSAL, K_END = 0, 128, 192, 320, 448, 832


def build(nc, A, out):
    scratch = nc.dram_tensor("t5_rows", [HEADS, T5W], F32, kind="Internal").ap()
    a_w_in, a_w_out = A["a_w_in"][0], A["a_w_out"][0]
    b_w_in, b_w_out = A["b_w_in"][0], A["b_w_out"][0]
    w_mod, w_qkv, w_o = A["w_mod"], A["w_qkv_2"], A["w_o_2"]
    ff1, ff3, ff2 = A["w1_2"][0], A["w3_2"][0], A["w2_2"][0]
    router = A["router_2"][0]

    units, at, unit_at = [], {}, {}

    def columns(name, w, blocks=None):
        at.setdefault(name, len(units))
        for cb in blocks or range(w.shape[1] // 512):
            for half in range(2):
                unit_at[name, cb, half] = len(units)
                rows, cols = slice(half * 512, half * 512 + 512), slice(cb * 512, cb * 512 + 512)
                units.append((w[rows, cols].rearrange("(c p) n -> p c n", p=P), 4))

    columns("mod0", w_mod[0])
    mod_after = [[0], [1], [2], [3], [4, 5]]
    for cb in range(5):
        columns("a_in", a_w_in, [cb])
        columns("mod1", w_mod[1], mod_after[cb])
    columns("a_out", a_w_out)
    columns("b_in", b_w_in)
    columns("b_out", b_w_out)
    columns("qkv0", w_qkv[0])
    columns("o0", w_o[0])
    at["ff"] = len(units)
    ff_at = {}

    def ff_unit(kind, j):
        ff_at[kind, j] = len(units)
        if kind == 2:
            units.append((ff2[j * 256:(j + 1) * 256, :].rearrange("(c p) n -> p c n", p=P), 2))
        else:
            w = ff1 if kind == 1 else ff3
            units.append((w[:, j * 256:(j + 1) * 256].rearrange("(c p) n -> p c n", p=P), 8))

    for j in range(HF):
        ff_unit(1, j)
        ff_unit(3, j)
        if j:
            ff_unit(2, j - 1)
    ff_unit(2, HF - 1)
    columns("qkv1", w_qkv[1])
    columns("o1", w_o[1])
    NS = len(units)
    blocks_of = {"a_in": [4] * 5, "a_out": [4] * 2, "b_in": [4] * 8, "b_out": [2] * 2, "qkv0": [4, 4, 4, 4, 2, 2],
                 "o0": [2] * 2, "qkv1": [4, 4, 4, 4, 2, 2], "o1": [2] * 2}
    group_engine, group_at = [], {}
    used_by = [None] * NS
    single = 0
    for name in ("mod0", "a_in", "a_out", "b_in", "b_out", "qkv0", "o0", "ff", "qkv1", "o1"):
        group_at[name] = len(group_engine)

        def mod_used(name, cb):
            for half in range(2):
                used_by[unit_at[name, cb, half]] = ("w_used", len([u for u in used_by if u and u[0] == "w_used"]) + 1)

        if name == "mod0":
            for cb in range(6):
                mod_used(name, cb)
            single = 12
            continue
        if name == "ff":
            for j in range(HF):
                for kind, who in ((1, "act"), (3, "dve")):
                    group_engine.append(who)
                    used_by[ff_at[kind, j]] = ("group_product_ready", len(group_engine))
                single += 1
                used_by[ff_at[2, j]] = ("w_used", single)
            continue
        for cb, n in enumerate(blocks_of[name]):
            single += 1
            group_engine += ["dve" if name[1:] in ("_out", "0", "1") else "act"] * n
            used_by[unit_at[name, cb, 0]] = ("w_used", single)
            used_by[unit_at[name, cb, 1]] = ("group_product_ready", len(group_engine))
            if name == "a_in":
                for c in mod_after[cb]:
                    mod_used("mod1", c)
                    single += 2
    last_unit = {k: unit_at[k, len(v) - 1, 1] for k, v in blocks_of.items()}
    last_unit["ff"] = ff_at[2, HF - 1]

    def emptied_by(g):
        return group_engine[g], group_engine[:g + 1].count(group_engine[g])

    top = ExitStack()
    with top:
        semaphores = {}

        def sem(name):
            if name not in semaphores:
                semaphores[name] = top.enter_context(nc.semaphore(name))
            return semaphores[name]

        def sb(name, shape, dt=F32, ctx=top):
            return ctx.enter_context(nc.sbuf_tensor(name, shape, dt))

        bank = [top.enter_context(nc.psum_tensor(f"bank{i}", [P, 512], F32)) for i in range(8)]

        raw = sb("raw", [P, NRAW, UW])
        w_hi = sb("w_hi", [P, NSPLIT, UW], F32R)
        w_lo = sb("w_lo", [P, NSPLIT, UW], F32R)
        xs = sb("xs", [P, 2 * TT, D])
        ident = sb("ident", [P, K_END])
        near, strict = ident[:, K_NEAR:K_STRICT], ident[:, K_STRICT:K_NEGS]
        negstrict, causal = ident[:, K_NEGS:K_CAUSAL], ident[:, K_CAUSAL:K_END]
        eye = ident[:, 0:P]
        vec_t = sb("vec_t", [P, NVEC])
        ones = sb("ones", [P, TOK])
        stat = sb("stat", [P, 16])
        qk_root = sb("qk_root", [P, 8])
        minus_half = sb("minus_half", [P, 8])
        diag = sb("diag", [P, 2 * TT, P])

        gate_b = sb("gate_b", [P, 2, D])
        route = sb("route", [P, 2 * P])
        spread = route[0:4, :]
        router_w = sb("router_w", [P, CH, EXP])

        ahead = ExitStack()
        with ExitStack() as bias_place:
            bias_b = sb("bias_b", [P, 2 * CH, 2 * TOK], F32, bias_place)
        h_hi = sb("h_hi", [P, CH, 2 * TOK], F32R, ahead)
        h_lo = sb("h_lo", [P, CH, 2 * TOK], F32R, ahead)
        prob = sb("prob", [P, 3, 512], F32, ahead)
        prob_t = sb("prob_t", [P, 2, 512], F32, ahead)
        work = sb("work", [P, 4, 512], F32, ahead)
        mod = sb("mod", [P, 2, 2 * CH, 2], F32, ahead)
        gain = sb("gain", [P, 2, CH, 2], F32, ahead)
        silu_c = sb("silu_c", [P, CH, 2], F32, ahead)
        negmax = sb("negmax", [P, 4, 4], F32, ahead)
        total = sb("total", [P, 4, 4], F32, ahead)
        inv = sb("inv", [P, 4, 4], F32, ahead)
        lay_a = ExitStack()
        ahead.enter_context(lay_a)
        q_a = sb("q_a", [P, PAIRS, 2 * TOK], F32, lay_a)
        k_a = sb("k_a", [P, KVH, 2 * TOK], F32, lay_a)
        v_a = sb("v_a", [P, 2 * TT, KVH * HD], F32, lay_a)
        z_a = sb("z_a", [P, CH, 2 * TOK], F32, lay_a)
        rope = sb("rope", [P, 4, TT, HD], F32, lay_a)
        qk_g = sb("qk_g", [P, 2, HD], F32, lay_a)
        mod_row = sb("mod_row", [4, 512], F32, lay_a)
        gate_row = sb("gate_row", [4, D], F32, lay_a)
        c_parts = sb("c_parts", [P, CH, 4], F32R, lay_a)
        lay_a.close()
        lay_b = ExitStack()
        q_b = sb("q_b", [P, PAIRS, TOK], F32, lay_b)
        k_b = sb("k_b", [P, PAIRS, 2 * TOK], F32, lay_b)
        v_b = sb("v_b", [P, 2 * TT, D], F32, lay_b)
        z_b = sb("z_b", [P, CH, TOK], F32, lay_b)
        lay_b.close()
        lay_2 = ExitStack()
        q_2 = sb("q_2", [P, PAIRS, TOK], F32, lay_2)
        k_2 = sb("k_2", [P, PAIRS, TOK], F32, lay_2)
        v_2 = sb("v_2", [P, TT, D], F32, lay_2)
        bias_t = sb("bias_t", [P, HEADS // 2, T5W], F32, lay_2)
        with ExitStack() as weights_place:
            softplus = sb("softplus", [P, 4, 512], F32, weights_place)
            stick = sb("stick", [P, 4, 512], F32, weights_place)
        hid_s = sb("hid_s", [P, 2, 512], F32, lay_2)
        hid_f = sb("hid_f", [P, 2, 512], F32, lay_2)
        hid_hi = sb("hid_hi", [P, 2, 512], F32R, lay_2)
        hid_lo = sb("hid_lo", [P, 2, 512], F32R, lay_2)
        lay_2.close()
        ahead.close()

        w_hi_x = sb("w_hi_x", [P, 3, UW], F32R)
        w_lo_x = sb("w_lo_x", [P, 3, UW], F32R)
        xe_hi = sb("xe_hi", [P, CH, P], F32R)
        xe_lo = sb("xe_lo", [P, CH, P], F32R)
        act_s = sb("act_s", [P, 512])
        act_f = sb("act_f", [P, 512])
        act_hi = sb("act_hi", [P, 512], F32R)
        act_lo = sb("act_lo", [P, 512], F32R)
        y_e = sb("y_e", [P, D])
        pick = sb("pick", [P, TT, P])
        pick_g = sb("pick_g", [P, TT, P])
        pick_gt = sb("pick_gt", [P, TOK])
        current = sb("current", [P, 6])
        visits = sb("visits", [P, EXP + MAXOVER + 1, 6])
        logit = sb("logit", [P, TT, EXP])
        best = sb("best", [P, TT, EXP])
        best_i = sb("best_i", [P, TT, EXP], U32)
        best_f = sb("best_f", [P, TT, 2])
        gates = sb("gates", [P, TT, 4])
        hot = sb("hot", [P, TT, 2, EXP])
        facts = sb("facts", [P, 6, EXP])
        over = sb("over", [P, 4, EXP])
        over_hot = sb("over_hot", [P, MAXOVER, EXP])
        over_tmp = sb("over_tmp", [P, MAXOVER, 6, EXP])
        ids_f = sb("ids_f", [P, 16])
        ids = sb("ids", [P, 16], I32)
        sb("gap_before_raw_x", [P, 1776])
        raw_x = sb("raw_x", [P, 3, UW])

        slots = [(0, 0), (0, 1), (1, 1), (1, 2), (1, 0), (0, 2)]

        def turned_token(t, half):
            return y_e[:, half * 512:(half + 1) * 512] if t == 0 else (act_s, act_f)[half][:]

        def ring6(base, more, n, a):
            part, slot = slots[n % 6]
            return (base, more)[part][:, slot, :].rearrange("p (a n) -> p a n", a=a)

        NJ = FE // 512
        visit_units = [(3, 0, 0), (3, 0, 1)]
        for j in range(1, NJ):
            visit_units += [(kind, jj, half) for kind, jj in ((1, j), (3, j), (2, j - 1)) for half in range(2)]
        visit_units += [(1, 0, 0), (1, 0, 1), (2, NJ - 1, 0), (2, NJ - 1, 1)]
        NV = len(visit_units)
        last_units = [u for u in visit_units if u[:2] != (1, 0)]
        LEAD = 2

        def visit_steps(last):
            return [(LEAD + k, *u) for k, u in enumerate(last_units if last else visit_units)]

        def x_done_in(name, t=TT - 1):
            return emptied["dve"], emptied_by(group_at[name] + sum(blocks_of[name]) - 1)[1] - (TT - 1 - t)

        def wait_used(eng, m):
            name, n = used_by[m]
            eng.wait_ge(sem(name), n)

        def unit_view(ring, n, a):
            return ring[:, n % NRAW, :].rearrange("p (a n) -> p a n", a=a)

        landed = [sem(f"weights_landed_{i}") for i in range(NRAW)]
        hi_ready, lo_ready, w_used = sem("w_hi_ready"), sem("w_lo_ready"), sem("w_used")
        x_landed = [sem(f"expert_weights_landed_{i}") for i in range(6)]
        x_raw_free, x_split_free = sem("x_raw_free"), sem("x_split_free")
        first_rest = [sem("first_rest_even"), sem("first_rest_odd")]
        x_hi_ready = sem("x_hi_ready")
        product = sem("group_product_ready")
        emptied = {"act": sem("bank_emptied_act"), "dve": sem("bank_emptied_dve")}

        def attention_plan():
            plans = {}
            ua = []
            for p in range(PAIRS):
                for t in range(TT):
                    for par in range(2):
                        ua.append((2 * p + par, [(t, t * P, 0, 2 * TOK, 0)], p))
            for p in range(PAIRS):
                for par in range(2):
                    ua.append((2 * p + par, [(t, TOK + t * P, TOK, TOK, t * TOK) for t in range(TT)], PAIRS + p))
            plans["a"] = ua
            plans["b"] = [u for u in ua if u[2] < PAIRS]
            plans["s"] = [(h, [(0, 0, 0, P, 0), (1, P, 0, TOK, P)], h // 2) for h in range(HEADS)]
            plans["m"] = plans["s"]
            return plans

        plans = attention_plan()
        LAG = {"a": 2, "b": 2, "s": 3, "m": 2}
        SPLIT_LAG = {"a": 4, "b": 4, "s": 5, "m": 4}

        def query_operand(st, h, q0):
            par = h % 2 * HD
            return {"a": q_a, "b": q_b}.get(st, q_2)[par:par + HD, h // 2, q0:q0 + P]

        def key_operand(st, h, k0, n):
            par = h % 2 * HD
            if st == "a":
                return k_a[par:par + HD, h // 4, k0:k0 + n]
            return (k_b if st == "b" else k_2)[par:par + HD, h // 2, k0:k0 + n]

        def value_operand(st, h, chunk):
            if st == "a":
                return v_a[:, chunk, h // 4 * HD:h // 4 * HD + HD]
            return (v_b if st == "b" else v_2)[:, chunk, h * HD:h * HD + HD]

        norm_tiles = {"n0": 4, "n1": 4, "f1": 2, "n2": 2, "n3": 2, "n4": 2, "n5": 2, "n6": 2}
        whole = ("n0", "n1", "n2", "n3", "n4")
        signals = {"squares": norm_tiles, "mean": {st: 1 for st in norm_tiles}, "root": {st: 1 for st in norm_tiles},
                   "diag": {st: norm_tiles[st] for st in whole}}
        for role in ("transposed", "h_full", "h_hi", "h_lo"):
            signals[role] = {st: CH for st in whole}
        signals["h_full"].update(n0=CH // 2, n1=CH // 2)
        for role in ("negmax", "exp"):
            signals[role] = {st: len(plans[st]) for st in "abm"}
        for role in ("scores", "prob", "prob_turned", "prob_t", "mixed"):
            signals[role] = {st: len(plans[st]) for st in "absm"}
        for role in ("gated", "out_hi", "out_lo"):
            signals[role] = {st: plans[st][-1][2] + 1 for st in "absm"}
        stage_sem = {role: sem(role) for role in signals}

        def reached(st, role, n):
            stages = list(signals[role])
            return stage_sem[role], sum(signals[role][s] for s in stages[:stages.index(st)]) + n

        S_BANK, T_BANK, O_BANK = {"a": [4, 5, 6, 3], "b": [4, 5, 6, 3], "s": [4, 5, 6, 3], "m": [4, 5, 6, 3]}, [7, 0], [1, 2]

        def near_bias(h):
            c = TT * (h % BIAS_RING)
            return bias_b[:, c:c + TT, TOK:2 * TOK]

        def t5_bias(h):
            if h < HEADS // 2:
                return [(0, 0, P, bias_t[:, h, 0:P]), (1, P, TOK, bias_t[:, h, P:T5W])]
            c = TT * (h - HEADS // 2)
            return [(0, 0, P, bias_b[:, c, TOK:TOK + P]), (1, P, TOK, bias_b[:, c + 1, TOK:2 * TOK])]

        def softplus_slot(h):
            return softplus[:, h % 4, 0:T5W]

        def weight_slot(h):
            return stick[:, h % 4, 0:T5W]

        def qk_slot(j):
            return z_a[:, 4 + j % 4, :]

        def mod_bank(l, cb):
            return bank[7 if l else 2 + cb % 2]

        def mod_row_of(cb):
            return mod_row[:] if cb < 4 else gate_row[:, (cb - 4) * 512:(cb - 3) * 512]

        def group_ends(st):
            u = plans[st]
            return {i: u[i][2] for i in range(len(u)) if i + 1 == len(u) or u[i + 1][2] != u[i][2]}

        def group_starts(st):
            u = plans[st]
            return {i: u[i][2] for i in range(len(u)) if i == 0 or u[i - 1][2] != u[i][2]}

        block = top.enter_context(nc.Block())

        @block.sync
        def _(sp):
            def load_unit(n):
                ap, a = units[n]
                if n >= NRAW:
                    sp.wait_ge(lo_ready, n - NRAW + 1)
                sp.dma_start(unit_view(raw, n, a), ap).then_inc(landed[n % NRAW], 16)

            def load_near_bias(heads):
                rpb = A["b_rpb"].tensor
                for h in heads:
                    if h >= BIAS_RING:
                        before = h - BIAS_RING
                        sp.wait_ge(sem("b_bias_used"), 4 * (before // 2) + 3 + before % 2)
                    for t in range(TT):
                        for half in range(2):
                            r = 2 * t + 1 - half
                            src = bass.AP(rpb, h * RPB_R * RPB_C + (7 - r) * RPB_C + 15 - (GRID_W - 1),
                                          [[1, GRID_W], [RPB_C, GROWS], [1, GRID_W]])
                            dst = near_bias(h)[half * GRID_W:(half + 1) * GRID_W, t, :]
                            sp.dma_start(dst.rearrange("p (r c) -> p r c", r=GROWS), src)\
                              .then_inc(sem(f"bias_landed_{h % BIAS_RING}"), 16)

            def load_t5_bias():
                sp.wait_ge(sem("t5_rows_stored"), 16)
                for h in range(HEADS):
                    for t, c0, n, dst in t5_bias(h):
                        src = bass.AP(scratch.tensor, h * T5W + P * (1 - t), [[1, P], [1, n]])
                        sp.dma_start(dst, src).then_inc(sem(f"bias_landed_{h % BIAS_RING}"), 16)

            def load_expert_unit(v, n, kind, j, half, e, first_six=False):
                if kind == 2:
                    src = A["e_w2_2"][0, e, j * 512:(j + 1) * 512, half * 512:(half + 1) * 512]
                else:
                    src = A["e_w1_2" if kind == 1 else "e_w3_2"][0, e, half * 512:(half + 1) * 512, j * 512:(j + 1) * 512]
                src = src.rearrange("a (c p) n -> p (a c) n", p=P) if len(src.shape) == 3 else src.rearrange("(c p) n -> p c n", p=P)
                if first_six and n >= 6:
                    who = n % 2
                    sp.wait_ge(first_rest[who], (n - 6) // 2 + 1)
                else:
                    sp.wait_ge(x_raw_free, v * NV + n + 1)
                sp.dma_start(ring6(raw, raw_x, n, 4), src).then_inc(x_landed[n % 6], 16)

            for n in range(NS):
                if n == at["b_out"] + 2:
                    wait_used(sp, unit_at["b_in", 5, 1])
                    load_near_bias(range(BIAS_RING))
                if n == at["b_out"] + 3:
                    load_near_bias(range(BIAS_RING, HEADS))
                if n == at["o0"]:
                    sp.wait_ge(sem("f1_x_done"), 2)
                    load_t5_bias()
                if n == at["o1"] + 3:
                    load_unit(n)
                    for half in range(2):
                        load_expert_unit(0, half, 1, 0, half, 0)
                    for m, kind, j, half in visit_steps(False)[:2]:
                        load_expert_unit(0, m, kind, j, half, 0)
                    continue
                load_unit(n)

            def load_visit(v, last):
                e = sp.value_load(ids[0:1, bass.ds(v, 1)], min_val=0, max_val=EXP - 1)
                e_next = None if last else sp.value_load(ids[0:1, bass.ds(v + 1, 1)], min_val=0, max_val=EXP - 1)
                for n, kind, j, half in visit_steps(last):
                    load_expert_unit(v, n, kind, j, half, bass.ds(e_next if (kind, j) == (1, 0) else e, 1))

            for n, kind, j, half in visit_steps(False)[2:-4]:
                load_expert_unit(0, n, kind, j, half, 0, n < 12)
            sp.wait_ge(sem("routed"), 1)
            last_visit = sp.value_load(ids[0:1, 12:13], min_val=EXP - 1, max_val=EXP + MAXOVER - 1)
            e_next = sp.value_load(ids[0:1, 1:2], min_val=0, max_val=EXP - 1)
            for n, kind, j, half in visit_steps(False)[-4:]:
                load_expert_unit(0, n, kind, j, half, bass.ds(e_next, 1) if (kind, j) == (1, 0) else 0)
            with sp.Fori(1, last_visit) as v:
                load_visit(v, False)
            with sp.Fori(last_visit, last_visit + 1) as v:
                load_visit(v, True)
            for t in range(TT):
                sp.wait_ge(sem("y_done"), t + 1)
                sp.dma_start(out[0, t * P:(t + 1) * P, :], xs[:, TT + t, :]).then_inc(sem("stored"), 16)
            sp.wait_ge(sem("stored"), 16 * TT)

        @block.scalar
        def _(act):
            state = {"split": 0}

            def load(dst, src, name, n=16):
                act.dma_start(dst, src).then_inc(sem(name), n)

            vec = work[:, 0, 0:P]
            rows = [(V_NORM, A["norm_g"].rearrange("l (c p) -> (l c) p", p=P)),
                    (V_BMOD, A["b_mod"].rearrange("l (c p) -> (l c) p", p=P)),
                    (V_MIX, A["mixer_norm_2"].rearrange("l (c p) -> (l c) p", p=P)),
                    (V_FFN, A["ffn_norm_2"].rearrange("l (c p) -> (l c) p", p=P)),
                    (V_C, A["c"].rearrange("l (c p) -> (l c) p", p=P)),
                    (V_C + CH, A["c_ctx"].rearrange("(c p) -> c p", p=P))]
            for r0, src in rows:
                load(vec[r0:r0 + src.shape[0], :], src, "vectors_landed")
            load(ident[:], A["keep"], "constants_landed")
            load(work[:, 1, 0:4 * HD], A["once"], "constants_landed")
            load(work[0:BUCKETS, 2, 0:T5W], A["onehot"], "t5_landed")
            load(work[0:BUCKETS, 3, 0:HEADS], A["rel_bias_2"], "t5_landed")
            load(qk_g[:, 0, :], bass.AP(A["a_q_norm_g"].tensor, 0, [[0, P], [1, HD]]), "qk_gain_landed")
            load(qk_g[:, 1, :], bass.AP(A["a_k_norm_g"].tensor, 0, [[0, P], [1, HD]]), "qk_gain_landed")
            load(spread[:], A["spread"], "spread_landed")
            load(xs[:, 0:TT, :], A["x"][0].rearrange("(t p) d -> p t d", p=P), "x_landed")
            load(xs[:, TT:2 * TT, :], A["ctx"][0].rearrange("(t p) d -> p t d", p=P), "x_landed")

            def split(upto):
                while state["split"] < min(upto, NS):
                    m = state["split"]
                    act.wait_ge(landed[m % NRAW], 16 * (m // NRAW + 1))
                    if m >= NSPLIT:
                        wait_used(act, m - NSPLIT)
                    nc.scalar.activation(w_hi[:, m % NSPLIT, :], raw[:, m % NRAW, :], ACT.Copy).then_inc(hi_ready, 1)
                    state["split"] += 1

            act.wait_ge(sem("t5_rows"), 1)
            nc.scalar.activation(prob[0:HEADS, 0, 0:T5W], bank[7][0:HEADS, 0:T5W], ACT.Copy).then_inc(sem("t5_copied"), 1)
            act.wait_ge(sem("t5_copied"), 1)
            act.dma_start(scratch, prob[0:HEADS, 0, 0:T5W]).then_inc(sem("t5_rows_stored"), 16)
            act.wait_ge(sem("vec_t_ready"), 1)
            nc.scalar.activation(silu_c[:].rearrange("p c w -> p w c"),
                                 vec_t[:, V_C:V_C + 2 * CH].rearrange("p (w c) -> p w c", w=2),
                                 ACT.Silu).then_inc(sem("silu_c_ready"), 1)
            act.wait_ge(sem("silu_c_ready"), 1)
            nc.scalar.activation(c_parts[:, :, 0:2], silu_c[:], ACT.Copy).then_inc(sem("c_hi_ready"), 1)

            def keep_mod_row(l, cb):
                wait_used(act, unit_at[f"mod{l}", cb, 1])
                if cb < 4 and l + cb:
                    act.wait_ge(sem("mod_turned"), 4 * l + cb)
                if cb >= 4 and l:
                    act.wait_ge(sem("gate_spread"), 4)
                nc.scalar.activation(mod_row_of(cb), mod_bank(l, cb)[0:4, :], ACT.Copy).then_inc(sem("mod_row_ready"), 1)


            def norm_squares(st, tiles, x_done):
                act.wait_ge(sem("t5_rows_stored"), 16)
                for t in range(tiles):
                    act.wait_ge(*x_done(t))
                    if t:
                        act.wait_ge(*reached(st, "squares", t))
                    nc.scalar.activation(prob[:, 0:2, :].rearrange("p a n -> p (a n)"), xs[:, t, :], ACT.Square,
                                         accum_out=stat[:, t:t + 1]).then_inc(stage_sem["squares"], 1)

            def norm(st, tiles, x_done, read_before):
                if x_done:
                    norm_squares(st, tiles, x_done)
                if read_before is not None:
                    wait_used(act, read_before)
                l = {"n0": 0, "n1": 1}.get(st)
                for c in range(CH):
                    if l is not None and c % 2:
                        act.wait_ge(*reached(st, "transposed", c + 1))
                        act.wait_ge(sem("gain_ready"), l + 1)
                        if c >= 2:
                            act.wait_ge(*reached(st, "h_lo", c - 1))
                        for w in range(tiles // TT):
                            cols = slice(w * TOK, (w + 1) * TOK)
                            last = nc.scalar.activation(work[:, c % 2, cols], bank[4 + c % 4][:, cols], ACT.Identity,
                                                        bias=mod[:, l, c, w:w + 1], scale=gain[:, l, c, w:w + 1])
                        last.then_inc(sem("h_full_odd"), 1)
                        act.wait_ge(sem("h_full_odd"), CH // 2 * l + c // 2 + 1)
                    else:
                        act.wait_ge(*reached(st, "h_full", c // 2 + 1 if l is not None else c + 1))
                    nc.scalar.activation(h_hi[:, c, 0:tiles * P], work[:, c % 2, 0:tiles * P], ACT.Copy).then_inc(stage_sem["h_hi"], 1)

            def linear(name, blocks, per_block, evac, after=None):
                g0 = group_at[name]
                for cb in range(blocks):
                    split(unit_at[name, cb, 1] + 3)
                    for i in range(per_block[cb]):
                        g = g0 + sum(per_block[:cb]) + i
                        act.wait_ge(product, g + 1)
                        evac(cb, i, bank[g % 4]).then_inc(emptied["act"], 1)
                    if after:
                        after(cb)

            def attention(st):
                plan, lag = plans[st], LAG[st]
                ends, n = group_ends(st), len(plan)
                if st == "s":
                    nc.scalar.preload_act_table_set("natural_log_exp_and_others")
                for i in range(n + SPLIT_LAG[st] + 1):
                    if i < n:
                        h, segs, _ = plan[i]
                        s = bank[S_BANK[st][i % len(S_BANK[st])]]
                        if st != "s" and i >= 3:
                            act.wait_ge(*reached(st, "prob_turned", i - 2))
                        if st == "s":
                            a = softplus_slot(i)
                            act.wait_ge(*reached("s", "scores", i + 1))
                            nc.scalar.activation(a, s[:, 0:T5W], ACT.Abs).then_inc(sem("s_abs"), 1)
                            act.wait_ge(sem("s_abs"), i + 1)
                            nc.scalar.activation(a, a, ACT.Exp, scale=-1.0).then_inc(sem("s_exp_abs"), 1)
                            act.wait_ge(sem("s_exp_abs"), i + 1)
                            nc.scalar.activation(a, a, ACT.Ln, bias=1.0).then_inc(sem("s_log1p"), 1)
                        else:
                            act.wait_ge(*reached(st, "negmax", i + 1))
                            for j, (t, q0, k0, nk, c0) in enumerate(segs):
                                last = nc.scalar.activation(prob[:, i % 3, c0:c0 + nk], s[:, c0:c0 + nk], ACT.Exp,
                                                            bias=negmax[:, i % 4, j:j + 1],
                                                            accum_out=total[:, i % 4, j:j + 1])
                            last.then_inc(stage_sem["exp"], 1)
                    if st == "s" and 1 <= i <= n:
                        act.wait_ge(sem("s_log_weight"), i)
                        nc.scalar.activation(weight_slot(i - 1), weight_slot(i - 1), ACT.Exp).then_inc(stage_sem["prob"], 1)
                    u = i - lag
                    if 0 <= u < n:
                        w = sum(x[3] for x in plan[u][1])
                        act.wait_ge(*reached(st, "prob_turned", u + 1))
                        if u >= 2:
                            act.wait_ge(*reached(st, "mixed", u - 1))
                        nc.scalar.activation(prob_t[:, u % 2, 0:w], bank[T_BANK[u % 2]][:, 0:w], ACT.Copy)\
                          .then_inc(stage_sem["prob_t"], 1)
                    u = i - SPLIT_LAG[st]
                    if u in ends:
                        p = ends[u]
                        act.wait_ge(*reached(st, "gated", p + 1))
                        nc.scalar.activation(out_hi(p, h_hi), gated_slot(p), ACT.Copy).then_inc(stage_sem["out_hi"], 1)

            for cb in range(6):
                split(at["mod0"] + 2 * cb + 4)
                keep_mod_row(0, cb)
                if cb == 2:
                    norm_squares("n0", 4, lambda t: (sem("x_landed"), 32))

            norm("n0", 4, None, None)

            def evac_a(cb, i, b):
                if cb < 3:
                    j = 4 * cb + i
                    if j >= 3:
                        act.wait_ge(sem("a_qk_normed"), j - 2)
                    if cb < 2:
                        return nc.scalar.activation(prob[:, j % 3, :], b[:], ACT.Copy)
                    nc.scalar.activation(v_a[:, i, :], b[:, 256:512], ACT.Copy)
                    return nc.scalar.activation(prob[:, j % 3, 0:256], b[:, 0:256], ACT.Copy)
                return nc.scalar.activation(z_a[:, (cb - 3) * 4 + i, :], b[:], ACT.Silu)

            def turn_a(cb):
                for c in mod_after[cb]:
                    for half in range(2):
                        split(unit_at["mod1", c, half] + 3)
                    keep_mod_row(1, c)
                if 1 <= cb <= 3:
                    for tt in range(4):
                        j = 4 * (cb - 1) + tt
                        act.wait_ge(sem("a_qk_turned"), j + 1)
                        src = bank[4 + j % 3][:].rearrange("p (c t) -> p c t", c=4)
                        cols = slice(tt * P, (tt + 1) * P)
                        if cb - 1 < 2:
                            last = nc.scalar.activation(q_a[:, (cb - 1) * 4:cb * 4, cols], src, ACT.Copy, scale=HD ** -0.5)
                        else:
                            last = nc.scalar.activation(k_a[:, :, cols], src, ACT.Copy)
                        last.then_inc(sem("a_qk_kept"), 1)

            def gated_slot(p):
                return work[:, 2 + p % 2, 0:TOK]

            def out_hi(p, ring):
                return ring[:, p % PAIRS, p // PAIRS * TOK:(p // PAIRS + 1) * TOK]

            linear("a_in", 5, [4] * 5, evac_a, turn_a)
            attention("a")
            split(at["a_out"] + 4)
            split(at["b_in"] + 2)

            norm("n1", 4, lambda t: (sem("a_x_done"), 5 + t), last_unit["a_out"])

            def flipped(b):
                return b[:, 0:TOK].rearrange("p (t n) -> p t n", t=TT)[:, :, ::-1]

            def evac_b(cb, i, b):
                c = cb % 2 * 4 + i
                if cb < 2:
                    return nc.scalar.activation(q_b[:, c, :].rearrange("p (t n) -> p t n", t=TT), flipped(b),
                                                ACT.Copy, scale=HD ** -0.5)
                if cb < 4:
                    return nc.scalar.activation(k_b[:, c, :], b[:], ACT.Copy)
                if cb < 6:
                    return nc.scalar.activation(v_b[:, i, (cb - 4) * 512:(cb - 3) * 512], b[:], ACT.Copy)
                return nc.scalar.activation(z_b[:, c, :], b[:, 0:TOK], ACT.Silu)

            linear("b_in", 8, [4] * 8, evac_b)
            attention("b")
            split(at["b_out"] + 4)
            split(at["qkv0"] + 2)
            for t in range(TT):
                act.wait_ge(sem("b_x_done"), 3 + t)
                if t:
                    act.wait_ge(*reached("f1", "squares", t))
                nc.scalar.activation(prob[:, 0:2, :].rearrange("p a n -> p (a n)"), xs[:, t, :], ACT.Square,
                                     accum_out=stat[:, t:t + 1]).then_inc(stage_sem["squares"], 1)

            def evac_qkv(flip):
                def evac(cb, i, b):
                    c = cb % 2 * 4 + i
                    if cb < 2:
                        src = flipped(b) if flip else b[:, 0:TOK].rearrange("p (t n) -> p t n", t=TT)
                        return nc.scalar.activation(q_2[:, c, :].rearrange("p (t n) -> p t n", t=TT), src,
                                                    ACT.Copy, scale=HD ** -0.5)
                    if cb < 4:
                        return nc.scalar.activation(k_2[:, c, :], b[:, 0:TOK], ACT.Copy)
                    return nc.scalar.activation(v_2[:, i, (cb - 4) * 512:(cb - 3) * 512], b[:], ACT.Copy)
                return evac

            norm("n2", 2, lambda t: (sem("f1_x_done"), 1 + t), last_unit["b_out"])
            linear("qkv0", 6, [4, 4, 4, 4, 2, 2], evac_qkv(False))
            attention("s")
            split(at["o0"] + 4)
            split(at["ff"] + 2)
            norm("n3", 2, lambda t: x_done_in("o0", t), last_unit["o0"])
            g0 = group_at["ff"]
            for j in range(HF):
                split(ff_at[1, j] + 3)
                act.wait_ge(product, g0 + 2 * j + 1)
                if j >= 2:
                    act.wait_ge(emptied["dve"], emptied_by(g0 + 2 * j - 3)[1])
                nc.scalar.activation(hid_s[:, j % 2, :], bank[(g0 + 2 * j) % 4][:], ACT.Silu).then_inc(emptied["act"], 1)
                split(ff_at[3, j] + 3)
                act.wait_ge(emptied["dve"], emptied_by(g0 + 2 * j + 1)[1])
                if j >= 2:
                    wait_used(act, ff_at[2, j - 2])
                nc.scalar.activation(hid_hi[:, j % 2, :], hid_f[:, j % 2, :], ACT.Copy).then_inc(sem("ff_hid_hi"), 1)
                split(ff_at[1, min(j + 1, HF - 1)] + 2)
            split(at["qkv1"] + 2)
            norm("n4", 2, lambda t: (sem("ff_x_done"), 2 * t + 2), last_unit["ff"])
            linear("qkv1", 6, [4, 4, 4, 4, 2, 2], evac_qkv(True))
            split(NS - 1)
            attention("m")
            split(NS)

            def squares(st, tiles, x_done, scratch):
                for t in range(tiles):
                    act.wait_ge(*x_done(t))
                    if t:
                        act.wait_ge(*reached(st, "squares", t))
                    nc.scalar.activation(scratch(t), xs[:, t, :], ACT.Square, accum_out=stat[:, t:t + 1]).then_inc(stage_sem["squares"], 1)

            def round_unit(v, n):
                act.wait_ge(x_landed[n % 6], v * (16 * NV // 6) + 16 * (n // 6 + 1))
                act.wait_ge(x_split_free, v * NV + n + 1)
                nc.scalar.activation(ring6(w_hi, w_hi_x, n, 1)[:, 0, :], ring6(raw, raw_x, n, 1)[:, 0, :], ACT.Copy).then_inc(x_hi_ready, 1)

            squares("n5", TT, lambda t: x_done_in("o1", t), lambda t: y_e[:])
            for n in range(3):
                round_unit(0, n)
            for t in range(TT):
                for half in range(2):
                    act.wait_ge(sem("n5_turned"), 2 * t + half + 1)
                    nc.scalar.activation(turned_token(t, half), bank[4 + 2 * t + half][:], ACT.Copy).then_inc(sem("n5_turned_kept"), 1)
            for n in range(3, 6):
                round_unit(0, n)
            act.wait_ge(sem("gap_ready"), 1)
            nc.scalar.activation(gates[:, :, 1], gates[:, :, 0], ACT.Exp).then_inc(sem("gap_exp"), 1)

            def gathered(n):
                for b in range(2):
                    act.wait_ge(sem("x_gathered"), 2 * n + b - 1)
                    nc.scalar.activation(xe_hi[:, 4 * b:4 * b + 4, :].rearrange("p c s -> p (c s)"), bank[6 + b][:], ACT.Copy)\
                      .then_inc(sem("xe_hi_ready"), 1)

            def first_silu(v):
                act.wait_ge(x_split_free, v * NV + LEAD + 6)
                nc.scalar.activation(act_s[:], bank[0][:], ACT.Silu).then_inc(sem("act_s_ready"), 1)

            gathered(1)
            round_unit(0, 6)
            first_silu(0)
            round_unit(0, 7)
            act.wait_ge(sem("routed"), 1)
            last_visit = act.value_load(ids[0:1, 12:13], min_val=EXP - 1, max_val=EXP + MAXOVER - 1)

            def visit(v, last):
                def turned(j):
                    act.wait_ge(sem("x_turned"), v * NJ + j + 1)
                    nc.scalar.activation(act_hi[:], bank[2][:], ACT.Copy).then_inc(sem("act_hi_ready"), 1)

                steps = visit_steps(last)
                for n, kind, j, half in steps:
                    if half and kind == 1 and j:
                        act.wait_ge(x_split_free, v * NV + n + 7)
                        act.wait_ge(sem("act_f_ready"), v * NJ + j)
                        nc.scalar.activation(act_s[:], bank[0][:], ACT.Silu).then_inc(sem("act_s_ready"), 1)
                        turned(j - 1)
                        if j == 2:
                            act.wait_ge(sem("pick_turned"), v + 1)
                            nc.scalar.activation(pick_gt[:], bank[3][:, 0:TOK], ACT.Copy).then_inc(sem("pick_gt_ready"), 1)
                    if half and kind == 1 and j == 0:
                        act.wait_ge(sem("act_f_ready"), v * NJ + NJ)
                        first_silu(v + 1)
                    if half and kind == 3 and j == NJ - 1 and not last:
                        gathered(v + 2)
                    if half and kind == 2 and j == NJ - 2:
                        turned(NJ - 1)
                    if kind == 2 and j == NJ - 1:
                        act.wait_ge(x_split_free, v * NV + n + 7)
                        nc.scalar.activation(y_e[:, half * 512:(half + 1) * 512], bank[4 + half][:], ACT.Copy).then_inc(sem("y_ready"), 1)
                    if (kind, j, half) in ((1, 0, 1), (2, NJ - 1, 0)):
                        continue
                    behind = [n] if (kind, j, half) != (2, NJ - 1, 1) else [n - 2, n - 1, n]
                    for m in behind:
                        if not last or m + 6 < NV:
                            round_unit(v, m + 6)

            with act.Fori(0, last_visit) as v:
                visit(v, False)
            with act.Fori(last_visit, last_visit + 1) as v:
                visit(v, True)

            squares("n6", TT, lambda t: (sem("x_added"), last_visit * 4 + 7 + t), lambda t: xs[:, TT + t, :])

        @block.vector
        def _(dve):
            state = {"split": 0}
            last_count = {}

            def then(ins, name):
                last_count[name] = last_count.get(name, 0) + 1
                ins.then_inc(sem(name), 1)
                dve.wait_ge(sem(name), last_count[name])

            def split(upto):
                while state["split"] < min(upto, NS):
                    m = state["split"]
                    dve.wait_ge(hi_ready, m + 1)
                    nc.vector.tensor_tensor(w_lo[:, m % NSPLIT, :], raw[:, m % NRAW, :],
                                            w_hi[:, m % NSPLIT, :].bitcast(F32), ALU.subtract).then_inc(lo_ready, 1)
                    state["split"] += 1

            nc.vector.memset(ones[:], 1.0).then_inc(sem("ones_ready"), 1)
            nc.vector.memset(minus_half[:], -0.5).then_inc(sem("ones_ready"), 1)
            dve.wait_ge(sem("vec_turned"), 1)
            nc.vector.tensor_copy(vec_t[:], bank[6][:, 0:NVEC]).then_inc(sem("vec_t_ready"), 1)
            dve.wait_ge(sem("vec_t_ready"), 1)
            dve.wait_ge(sem("constants_landed"), 32)
            dve.wait_ge(sem("qk_gain_landed"), 32)
            for w in range(2):
                for t in range(TT):
                    cos = work[:, 1, t * HD:(t + 1) * HD]
                    sin = work[:, 1, (TT + t) * HD:(TT + t + 1) * HD]
                    nc.vector.tensor_tensor(rope[:, 2 * w, t, :], cos, qk_g[:, w, :], ALU.mult)
                    g4 = qk_g[:, w, :].rearrange("p (a h i) -> p a h i", a=2, h=2)
                    s4 = sin.rearrange("p (a h i) -> p a h i", a=2, h=2)
                    o4 = rope[:, 2 * w + 1, t, :].rearrange("p (a h i) -> p a h i", a=2, h=2)
                    for half in range(2):
                        last = nc.vector.tensor_tensor(o4[:, :, half, :], s4[:, :, half, :], g4[:, :, 1 - half, :], ALU.mult)
            last.then_inc(sem("rope_ready"), 1)

            dve.wait_ge(sem("c_hi_ready"), 1)
            nc.vector.tensor_tensor(c_parts[:, :, 2:4], silu_c[:], c_parts[:, :, 0:2].bitcast(F32), ALU.subtract)\
              .then_inc(sem("c_parts_ready"), 1)

            def add_mod_bias(l, cb):
                dve.wait_ge(sem("mod_turned"), 4 * l + cb + 1)
                b = vec_t[:, V_BMOD + 24 * l + 4 * cb:V_BMOD + 24 * l + 4 * cb + 4]
                nc.vector.tensor_tensor(mod[:, l, 4 * cb:4 * cb + 4, :], mod_bank(l, cb)[:, 0:8].rearrange("p (c w) -> p c w", w=2),
                                        b.unsqueeze(2).broadcast_to([P, 4, 2]), ALU.add).then_inc(sem("mod_ready"), 1)

            def gains(l):
                dve.wait_ge(sem("mod_ready"), 4 * l + 4)
                for w in range(2):
                    last = nc.vector.scalar_tensor_tensor(gain[:, l, :, w], mod[:, l, CH:2 * CH, w], 1.0,
                                                          vec_t[:, V_NORM + CH * l:V_NORM + CH * (l + 1)], ALU.add, ALU.mult)
                last.then_inc(sem("gain_ready"), 1)
                dve.wait_ge(sem("gain_ready"), l + 1)

            def roots(st, tiles):
                dve.wait_ge(*reached(st, "squares", tiles))
                v, r = stat[:, 4:4 + tiles], stat[:, 8:8 + tiles]
                nc.vector.tensor_scalar(v, stat[:, 0:tiles], 1.0 / D, EPS, ALU.mult, ALU.add).then_inc(stage_sem["mean"], 1)
                dve.wait_ge(*reached(st, "root", 1))
                return r

            def norm_diag(st, tiles):
                r = roots(st, tiles)
                for t in range(tiles):
                    nc.vector.tensor_scalar(diag[:, t, :], eye, r[:, t:t + 1], None, ALU.mult).then_inc(stage_sem["diag"], 1)

            def norm(st, tiles, scale, shift, read_before):
                if st != "n0":
                    norm_diag(st, tiles)
                if read_before is not None:
                    wait_used(dve, read_before)
                width = tiles * P

                shared = shift is not None

                def rest(c):
                    dve.wait_ge(*reached(st, "h_hi", c + 1))
                    if not (shared and c % 2):
                        dve.wait_ge(*reached(st, "h_full", c // 2 + 1 if shared else c + 1))
                    nc.vector.tensor_tensor(h_lo[:, c, 0:width], work[:, c % 2, 0:width],
                                            h_hi[:, c, 0:width].bitcast(F32), ALU.subtract).then_inc(stage_sem["h_lo"], 1)

                for c in range(CH):
                    if shared and c % 2:
                        rest(c - 1)
                        continue
                    dve.wait_ge(*reached(st, "transposed", c + 1))
                    if c >= 2:
                        dve.wait_ge(*reached(st, "h_lo", c - 1))
                    for w in range(tiles // TT):
                        cols = slice(w * TOK, (w + 1) * TOK)
                        if shift:
                            last = nc.vector.tensor_scalar(work[:, c % 2, cols], bank[4 + c % 4][:, cols], scale(c, w),
                                                           shift(c, w), ALU.mult, ALU.add)
                        else:
                            last = nc.vector.tensor_scalar(work[:, c % 2, cols], bank[4 + c % 4][:, cols], scale(c, w),
                                                           None, ALU.mult)
                    last.then_inc(stage_sem["h_full"], 1)
                    if c:
                        rest(c - 1)
                rest(CH - 1)

            def add_gates(n0, n1):
                for n in range(n0, n1):
                    dve.wait_ge(sem("gate_spread"), n + 1)
                    if n < 4:
                        dve.wait_ge(sem("gate_bias_landed"), 32)
                    else:
                        dve.wait_ge(sem("gate_bias_1_landed"), 16)
                    g = gate_b[:, n // 2 % 2, n % 2 * 512:(n % 2 + 1) * 512]
                    nc.vector.tensor_tensor(g, bank[4 + n % 4][:], g, ALU.add).then_inc(sem("gate_ready"), 1)

            def attention(st, gate, read_before):
                plan, lag = plans[st], LAG[st]
                ends, n = group_ends(st), len(plan)
                wait_used(dve, read_before)

                def finish(i):
                    u = i - lag - 2
                    if u in ends:
                        p = ends[u]
                        dve.wait_ge(*reached(st, "mixed", u + 1))
                        if p >= 2:
                            dve.wait_ge(*reached(st, "out_hi", p - 1))
                            dve.wait_ge(*reached(st, "out_lo", p - 1))
                        b = bank[O_BANK[p % 2]]
                        o = work[:, 2 + p % 2, 0:TOK]
                        if gate:
                            ins = gate(p, b, o)
                        else:
                            ins = nc.vector.tensor_copy(o, b[:, 0:TOK])
                        ins.then_inc(stage_sem["gated"], 1)
                    u = i - SPLIT_LAG[st] - 1
                    if u in ends:
                        p = ends[u]
                        dst = h_lo[:, p % PAIRS, p // PAIRS * TOK:(p // PAIRS + 1) * TOK]
                        hi = h_hi[:, p % PAIRS, p // PAIRS * TOK:(p // PAIRS + 1) * TOK]
                        dve.wait_ge(*reached(st, "out_hi", p + 1))
                        dve.wait_ge(*reached(st, "gated", p + 1))
                        nc.vector.tensor_tensor(dst, work[:, 2 + p % 2, 0:TOK], hi.bitcast(F32), ALU.subtract)\
                          .then_inc(stage_sem["out_lo"], 1)

                for i in range(n + SPLIT_LAG[st] + 2):
                    if st == "s":
                        finish(i)
                    if i < n:
                        h, segs, _ = plan[i]
                        s = bank[S_BANK[st][i % len(S_BANK[st])]]
                        dve.wait_ge(*reached(st, "scores", i + 1))
                        if st == "s":
                            w = T5W
                            a, o = softplus_slot(i), weight_slot(i)
                            dve.wait_ge(sem("s_log1p"), i + 1)
                            then(nc.vector.scalar_tensor_tensor(a, s[:, 0:w], 0.0, a, ALU.max, ALU.add), "s_full_softplus")
                            if i >= 4:
                                dve.wait_ge(*reached("s", "prob_turned", i - 3))
                            nc.vector.tensor_tensor_scan(o[:, P - 1::-1], ones[:, 0:P], a[:, P - 1::-1], 0.0, ALU.mult, ALU.add)
                            ins = nc.vector.tensor_tensor_scan(o[:, w - 1:P - 1:-1], ones[:, 0:TOK], a[:, w - 1:P - 1:-1], 0.0,
                                                               ALU.mult, ALU.add)
                            ins.then_inc(sem("s_softplus"), 1)
                            dve.wait_ge(sem("s_softplus"), i + 1)
                            nc.vector.tensor_tensor(o, s[:, 0:w], o, ALU.subtract).then_inc(sem("s_log_weight"), 1)
                        else:
                            if st == "b":
                                dve.wait_ge(sem("b_bias_ready"), h + 1)
                                ins = nc.vector.tensor_tensor(s[:, 0:TOK], s[:, 0:TOK], near_bias(h)[:, segs[0][0], :], ALU.add)
                                ins.then_inc(sem("b_bias_used"), 1)
                                dve.wait_ge(sem("b_bias_used"), i + 1)
                            if st == "m":
                                dve.wait_ge(sem("m_bias_ready"), h + 1)
                                for t, c0, nk, b in t5_bias(h):
                                    ins = nc.vector.tensor_tensor(s[:, c0:c0 + nk], s[:, c0:c0 + nk], b, ALU.add)
                                ins.then_inc(sem("m_bias_used"), 1)
                                dve.wait_ge(sem("m_bias_used"), i + 1)
                            if i >= 4:
                                dve.wait_ge(*reached(st, "exp", i - 3))
                            for j, (t, q0, k0, nk, c0) in enumerate(segs):
                                last = nc.vector.tensor_reduce(negmax[:, i % 4, j:j + 1], s[:, c0:c0 + nk], AX.X, ALU.max, negate=True)
                            last.then_inc(stage_sem["negmax"], 1)
                    u = i - 1
                    if st != "s" and 0 <= u < n:
                        segs = plan[u][1]
                        dve.wait_ge(*reached(st, "exp", u + 1))
                        then(nc.vector.reciprocal(inv[:, u % 4, 0:len(segs)], total[:, u % 4, 0:len(segs)]), "inv")
                        for j, (t, q0, k0, nk, c0) in enumerate(segs):
                            pr = prob[:, u % 3, c0:c0 + nk]
                            last = nc.vector.tensor_scalar(pr, pr, inv[:, u % 4, j:j + 1], None, ALU.mult)
                        last.then_inc(stage_sem["prob"], 1)
                    if st != "s":
                        finish(i)

            def residual(name, st, tiles, gates):
                g0 = group_at[name]
                for cb in range(2):
                    split(at[name] + 2 * cb + 4)
                    cols = slice(cb * 512, (cb + 1) * 512)
                    for t in range(tiles):
                        g = g0 + cb * tiles + t
                        dve.wait_ge(product, g + 1)
                        x = xs[:, t, cols]
                        if gates:
                            tmp = work[:, g % 2, :]
                            if g - g0 >= 2:
                                dve.wait_ge(sem(st + "_x_done"), g - g0 - 1)
                            ins = nc.vector.tensor_tensor(tmp, bank[g % 4][:], gate_b[:, gates(t), cols], ALU.mult)
                            ins.then_inc(emptied["dve"], 1)
                            dve.wait_ge(emptied["dve"], emptied_by(g)[1])
                            ins = nc.vector.tensor_tensor(x, x, tmp, ALU.add)
                        else:
                            ins = nc.vector.tensor_tensor(x, x, bank[g % 4][:], ALU.add)
                            ins.then_inc(emptied["dve"], 1)
                            continue
                        ins.then_inc(sem(st + "_x_done"), 1)

            for cb in range(6):
                split(at["mod0"] + 2 * cb + 4)
                if cb < 4:
                    add_mod_bias(0, cb)
                if cb == 3:
                    norm_diag("n0", 4)
            gains(0)

            norm("n0", 4, lambda c, w: gain[:, 0, c, w:w + 1], lambda c, w: mod[:, 0, c, w:w + 1], None)
            for cb in range(5):
                split(unit_at["a_in", cb, 1] + 3)
                if cb == 0:
                    add_gates(0, 4)
                ahead_to = unit_at["a_in", cb + 1, 1] + 1 if cb < 4 else at["a_out"] + 2
                if cb >= 3:
                    split(ahead_to)
                    if cb == 3:
                        add_mod_bias(1, cb)
                    continue
                heads = 8 if cb < 2 else 4
                w = heads * HD
                for tt in range(4):
                    j = 4 * cb + tt
                    sq, qn = prob_t[:, 0, 0:w], work[:, 0, 0:w]
                    src = prob[:, j % 3, 0:w]
                    dst = qk_slot(j)
                    dve.wait_ge(emptied["act"], group_at["a_in"] + j + 1)
                    if j:
                        dve.wait_ge(sem("a_qk_done"), j)
                    then(nc.vector.tensor_tensor(sq, src, src, ALU.mult), "a_qk_square")
                    ss, v, r = stat[:, 0:heads], stat[:, 8:8 + heads], qk_root[:, 0:heads]
                    per_head = lambda ap: ap.rearrange("p (h d) -> p h d", d=HD)
                    then(nc.vector.tensor_reduce(ss, per_head(sq), AX.X, ALU.add), "a_qk_sum")
                    nc.vector.tensor_scalar(v, ss, 1.0 / HD, EPS, ALU.mult, ALU.add).then_inc(sem("a_qk_mean"), 1)
                    dve.wait_ge(sem("a_qk_root"), j + 1)
                    ins = nc.vector.tensor_tensor(per_head(qn), per_head(src), r.unsqueeze(2).broadcast_to([P, heads, HD]), ALU.mult)
                    ins.then_inc(sem("a_qk_normed"), 1)
                    dve.wait_ge(sem("a_qk_normed"), j + 1)
                    if j >= 4:
                        dve.wait_ge(sem("a_qk_turned"), j - 3)
                    outs = [per_head(dst)] if cb < 2 else [dst.rearrange("p (h u d) -> p h u d", u=2, d=HD)[:, :, u, :] for u in range(2)]
                    kind = 0 if cb < 2 else 1
                    if tt < TT:
                        dve.wait_ge(sem("rope_ready"), 1)
                        t1, t2 = prob_t[:, 0, 0:w], work[:, 1, 0:w]
                        by_head = lambda ap: ap.unsqueeze(1).broadcast_to([P, heads, HD])
                        nc.vector.tensor_tensor(per_head(t1), per_head(qn), by_head(rope[:, 2 * kind, tt, :]), ALU.mult)
                        five = lambda ap: ap.rearrange("p (h i) -> p h i", i=16)
                        sgn = rope[:, 2 * kind + 1, tt, :].rearrange("p (a b i) -> p a b i", a=2, b=2)
                        q5 = qn.rearrange("p (h a b i) -> p h a b i", a=2, b=2, i=16)
                        o5 = t2.rearrange("p (h a b i) -> p h a b i", a=2, b=2, i=16)
                        for a in range(2):
                            for half in range(2):
                                ins = nc.vector.tensor_tensor(o5[:, :, a, half, :], q5[:, :, a, 1 - half, :],
                                                              sgn[:, a, half, :].unsqueeze(1).broadcast_to([P, heads, 16]), ALU.mult)
                        then(ins, "a_qk_rotated")
                        for o in outs:
                            ins = nc.vector.tensor_tensor(o, per_head(t1), per_head(t2), ALU.add)
                    else:
                        for o in outs:
                            ins = nc.vector.tensor_tensor(o, per_head(qn), qk_g[:, kind, :].unsqueeze(1).broadcast_to([P, heads, HD]), ALU.mult)
                    ins.then_inc(sem("a_qk_done"), 1)
                    split(min(state["split"] + 1, ahead_to))
                add_mod_bias(1, cb)

            def gate_a(p, b, o):
                w = p // PAIRS
                return nc.vector.tensor_tensor(o, b[:, 0:TOK], z_a[:, p % PAIRS, w * TOK:(w + 1) * TOK], ALU.mult)

            dve.wait_ge(emptied["act"], group_at["a_out"])
            attention("a", gate_a, last_unit["a_in"])
            gains(1)
            dve.wait_ge(sem("gate_ready"), 4)
            residual("a_out", "a", 4, lambda t: t // TT)

            norm("n1", 4, lambda c, w: gain[:, 1, c, w:w + 1], lambda c, w: mod[:, 1, c, w:w + 1], last_unit["a_out"])
            for cb in range(8):
                split(at["b_in"] + 2 * cb + 4)
                if cb == 0:
                    add_gates(4, 6)
            def gate_bx(p, b, o):
                unflip = lambda ap: ap.rearrange("p (t n) -> p t n", t=TT)
                return nc.vector.tensor_tensor(unflip(o), unflip(b[:, 0:TOK])[:, :, ::-1], unflip(z_b[:, p, :]), ALU.mult)

            dve.wait_ge(emptied["act"], emptied_by(group_at["b_in"] + 31)[1])
            attention("b", gate_bx, last_unit["b_in"])
            dve.wait_ge(sem("gate_ready"), 6)
            residual("b_out", "b", 2, lambda t: 0)
            r = roots("f1", TT)
            dve.wait_ge(sem("final_gain_landed"), 16)
            for t in range(TT):
                nc.vector.scalar_tensor_tensor(xs[:, t, :], xs[:, t, :], r[:, t:t + 1], gate_b[:, 1, :], ALU.mult, ALU.mult)\
                  .then_inc(sem("f1_x_done"), 1)
            dve.wait_ge(sem("f1_x_done"), 2)

            norm("n2", 2, lambda c, w: vec_t[:, V_MIX + c:V_MIX + c + 1], None, last_unit["b_out"])
            for cb in range(6):
                split(at["qkv0"] + 2 * cb + 4)
            attention("s", None, last_unit["qkv0"])
            residual("o0", "o0", 2, None)
            norm("n3", 2, lambda c, w: vec_t[:, V_FFN + c:V_FFN + c + 1], None, last_unit["o0"])
            g0 = group_at["ff"]
            for j in range(HF):
                split(ff_at[1, j] + 3)
                split(ff_at[3, j] + 3)
                dve.wait_ge(product, g0 + 2 * j + 2)
                dve.wait_ge(emptied["act"], emptied_by(g0 + 2 * j)[1])
                if j >= 2:
                    dve.wait_ge(sem("ff_hid_hi"), j - 1)
                    dve.wait_ge(sem("ff_hid_lo"), j - 1)
                nc.vector.tensor_tensor(hid_f[:, j % 2, :], hid_s[:, j % 2, :], bank[(g0 + 2 * j + 1) % 4][:], ALU.mult)\
                  .then_inc(emptied["dve"], 1)
                dve.wait_ge(emptied["dve"], emptied_by(g0 + 2 * j + 1)[1])
                dve.wait_ge(sem("ff_hid_hi"), j + 1)
                if j >= 2:
                    wait_used(dve, ff_at[2, j - 2])
                nc.vector.tensor_tensor(hid_lo[:, j % 2, :], hid_f[:, j % 2, :], hid_hi[:, j % 2, :].bitcast(F32), ALU.subtract)\
                  .then_inc(sem("ff_hid_lo"), 1)
                split(ff_at[1, min(j + 1, HF - 1)] + 2)
            split(at["qkv1"] + 2)
            for t in range(TT):
                for half in range(2):
                    if (t, half) == (1, 1):
                        wait_used(dve, last_unit["ff"])
                    else:
                        dve.wait_ge(sem("ff_out_ready"), 2 * t + half + 1)
                    x = xs[:, t, half * 512:(half + 1) * 512]
                    nc.vector.tensor_tensor(x, x, bank[4 + 2 * t + half][:], ALU.add).then_inc(sem("ff_x_done"), 1)
            dve.wait_ge(sem("ff_x_done"), 4)
            norm("n4", 2, lambda c, w: vec_t[:, V_MIX + CH + c:V_MIX + CH + c + 1], None, last_unit["ff"])
            for cb in range(6):
                split(at["qkv1"] + 2 * cb + 4)

            def unflip_copy(p, b, o):
                unflip = lambda ap: ap.rearrange("p (t n) -> p t n", t=TT)
                return nc.vector.tensor_copy(unflip(o), unflip(b[:, 0:TOK])[:, :, ::-1])

            split(NS - 1)
            dve.wait_ge(lo_ready, NS - 1)
            for i in range(4):
                dve.nop().then_inc(x_raw_free, 1)
            attention("m", unflip_copy, last_unit["qkv1"])
            dve.wait_ge(sem("m_bias_used"), HEADS)
            dve.nop().then_inc(x_raw_free, 1)
            split(NS)
            dve.wait_ge(lo_ready, NS)
            dve.nop().then_inc(x_raw_free, 1)
            residual("o1", "o1", 2, None)
            dve.wait_ge(*x_done_in("o1"))
            for i in range(4):
                dve.nop().then_inc(sem("x_added"), 1)

            chain = [0]

            def link(ins):
                chain[0] += 1
                ins.then_inc(sem("routing_step"), 1)
                dve.wait_ge(sem("routing_step"), chain[0])

            r = roots("n5", TT)
            dve.wait_ge(sem("ffn_gain_landed"), 16)
            for t in range(TT):
                nc.vector.scalar_tensor_tensor(xs[:, TT + t, :], xs[:, t, :], r[:, t:t + 1], gate_b[:, 0, :], ALU.mult, ALU.mult)\
                  .then_inc(sem("n5_h_ready"), 1)
            def rest_unit(v, n):
                dve.wait_ge(x_hi_ready, v * NV + n + 1)
                nc.vector.tensor_tensor(ring6(w_lo, w_lo_x, n, 1)[:, 0, :], ring6(raw, raw_x, n, 1)[:, 0, :],
                                        ring6(w_hi, w_hi_x, n, 1)[:, 0, :].bitcast(F32), ALU.subtract).then_inc(x_raw_free, 1)

            def first_rests(n):
                dve.wait_ge(x_hi_ready, n + 1)
                nc.vector.tensor_tensor(ring6(w_lo, w_lo_x, n, 1)[:, 0, :], ring6(raw, raw_x, n, 1)[:, 0, :],
                                        ring6(w_hi, w_hi_x, n, 1)[:, 0, :].bitcast(F32), ALU.subtract).then_inc(first_rest[1], 1)

            first_rests(1)
            link(nc.vector.memset(visits[:], 0.0))
            link(nc.vector.memset(ids_f[:], 0.0))
            dve.wait_ge(sem("route_landed"), 32)
            count = route[:, P:P + EXP]
            first_rests(3)
            for t in range(TT):
                if t:
                    first_rests(5)
                dve.wait_ge(sem("logits"), t + 1)
                link(nc.vector.tensor_copy(logit[:, t, :], bank[3 * (1 - t)][:, 0:EXP]))
                link(nc.vector.max(best[:, t, :], logit[:, t, :]))
                link(nc.vector.max_index(best_i[:, t, :], best[:, t, :], logit[:, t, :]))
            link(nc.vector.tensor_copy(best_f[:], best_i[:, :, 0:2]))
            link(nc.vector.tensor_tensor(hot[:], count.unsqueeze(1).unsqueeze(1).broadcast_to([P, TT, 2, EXP]),
                                         best_f[:].unsqueeze(3).broadcast_to([P, TT, 2, EXP]), ALU.is_equal))
            nc.vector.tensor_tensor(facts[:, 2:4, :], hot[:, :, 0, :], hot[:, :, 1, :], ALU.add).then_inc(sem("chosen"), 1)
            nc.vector.tensor_tensor(gates[:, :, 0], best[:, :, 1], best[:, :, 0], ALU.subtract).then_inc(sem("gap_ready"), 1)
            dve.wait_ge(sem("slots"), 3)
            for t in range(TT):
                link(nc.vector.tensor_copy(facts[:, t, :], bank[1 + t][:, 0:EXP]))
            for t in range(TT):
                ins = nc.vector.tensor_scalar(pick[:, t, :], route[:, P:2 * P], facts[:, t, 0:1], facts[:, 2 + t, 0:1], ALU.is_equal, ALU.mult)
            ins.then_inc(sem("pick_ready"), 1)
            dve.wait_ge(sem("pick_ready"), 1)
            dve.wait_ge(sem("gap_exp"), 1)
            link(nc.vector.tensor_scalar(gates[:, :, 2], gates[:, :, 1], 1.0, None, ALU.add))
            link(nc.vector.reciprocal(gates[:, :, 2], gates[:, :, 2]))
            link(nc.vector.tensor_tensor(gates[:, :, 3], gates[:, :, 1], gates[:, :, 2], ALU.mult))
            for t in range(TT):
                link(nc.vector.tensor_scalar(facts[:, 4 + t, :], hot[:, t, 0, :], gates[:, t, 2:3], None, ALU.mult))
                link(nc.vector.scalar_tensor_tensor(facts[:, 4 + t, :], hot[:, t, 1, :], gates[:, t, 3:4], facts[:, 4 + t, :], ALU.mult, ALU.add))
            for t in range(TT):
                ins = nc.vector.tensor_scalar(pick_g[:, t, :], pick[:, t, :], facts[:, 4 + t, 0:1], None, ALU.mult)
            ins.then_inc(sem("pick_g_ready"), 1)

            def gathered(n):
                for b in range(2):
                    dve.wait_ge(sem("xe_hi_ready"), 2 * n + b - 1)
                    cols = slice(4 * b, 4 * b + 4)
                    nc.vector.tensor_tensor(xe_lo[:, cols, :].rearrange("p c s -> p (c s)"), bank[6 + b][:],
                                            xe_hi[:, cols, :].rearrange("p c s -> p (c s)").bitcast(F32), ALU.subtract)\
                      .then_inc(sem("xe_lo_ready"), 1)

            gathered(1)
            link(nc.vector.tensor_copy(over[:, 0, :], bank[4][:, 0:EXP]))
            link(nc.vector.tensor_copy(visits[:, 0:EXP, :], facts[:].rearrange("p q e -> p e q")))
            link(nc.vector.tensor_scalar(over[:, 1, :], over[:, 0, :], float(P), None, ALU.is_gt))
            link(nc.vector.tensor_tensor_scan(over[:, 2, :], ones[:, 0:EXP], over[:, 1, :], 0.0, ALU.mult, ALU.add))
            link(nc.vector.tensor_tensor(over[:, 3, :], over[:, 2, :], over[:, 1, :], ALU.subtract))
            for i in range(MAXOVER):
                link(nc.vector.scalar_tensor_tensor(over_hot[:, i, :], over[:, 3, :], float(i), over[:, 1, :], ALU.is_equal, ALU.mult))
                for q in range(6):
                    ins = nc.vector.tensor_tensor(over_tmp[:, i, q, :], over_hot[:, i, :], facts[:, q, :], ALU.mult)
                link(ins)
            link(nc.vector.tensor_reduce(visits[:, EXP:EXP + MAXOVER, :], over_tmp[:], AX.X, ALU.add))
            link(nc.vector.tensor_scalar(visits[:, EXP:EXP + MAXOVER, 0:TT], visits[:, EXP:EXP + MAXOVER, 0:TT], -float(P), None, ALU.add))
            for i in range(MAXOVER):
                ins = nc.vector.tensor_tensor(over_tmp[:, i, 0, :], over_hot[:, i, :], count, ALU.mult)
            link(ins)
            link(nc.vector.tensor_copy(ids_f[:, 0:EXP], count))
            link(nc.vector.tensor_reduce(ids_f[:, EXP:EXP + MAXOVER], over_tmp[:, :, 0, :], AX.X, ALU.add))
            link(nc.vector.tensor_scalar(ids_f[:, 12:13], over[:, 2, EXP - 1:EXP], float(EXP - 1), None, ALU.add))
            nc.vector.tensor_copy(ids[:], ids_f[:]).then_inc(sem("routed"), 1)

            def picks(v):
                nc.vector.tensor_scalar(current[:], visits[:, bass.ds(v, 1), :].rearrange("p a q -> p (a q)"), 0.0, None, ALU.add)\
                  .then_inc(sem("current_ready"), 1)
                dve.wait_ge(sem("current_ready"), v)
                for t in range(TT):
                    ins = nc.vector.tensor_scalar(pick[:, t, :], route[:, P:2 * P], current[:, t:t + 1], current[:, 2 + t:3 + t],
                                                  ALU.is_equal, ALU.mult)
                ins.then_inc(sem("pick_ready"), 1)
                dve.wait_ge(sem("pick_ready"), v + 1)
                for t in range(TT):
                    ins = nc.vector.tensor_scalar(pick_g[:, t, :], pick[:, t, :], current[:, 4 + t:5 + t], None, ALU.mult)
                ins.then_inc(sem("pick_g_ready"), 1)

            for who in range(2):
                dve.wait_ge(first_rest[who], 3)
            for n in range(6):
                dve.nop().then_inc(x_raw_free, 1)
            rest_unit(0, 6)
            rest_unit(0, 7)
            dve.wait_ge(sem("routed"), 1)
            last_visit = dve.value_load(ids[0:1, 12:13], min_val=EXP - 1, max_val=EXP + MAXOVER - 1)

            def visit(v, last):
                def turned(j):
                    dve.wait_ge(sem("act_hi_ready"), v * NJ + j + 1)
                    nc.vector.tensor_tensor(act_lo[:], bank[2][:], act_hi[:].bitcast(F32), ALU.subtract).then_inc(sem("act_lo_ready"), 1)

                for n, kind, j, half in visit_steps(last):
                    if half and kind == 1 and j:
                        turned(j - 1)
                    if half and kind == 3:
                        dve.wait_ge(x_split_free, v * NV + n + 7)
                        dve.wait_ge(sem("act_s_ready"), v * NJ + j + 1)
                        nc.vector.tensor_tensor(act_f[:], act_s[:], bank[1][:], ALU.mult).then_inc(sem("act_f_ready"), 1)
                        if j == 3 and not last:
                            dve.wait_ge(sem("pick_turned"), v + 1)
                            picks(v + 1)
                        if j == NJ - 1 and not last:
                            gathered(v + 2)
                    if half and kind == 2 and j == NJ - 2:
                        turned(NJ - 1)
                    if not last or n + 6 < NV:
                        rest_unit(v, n + 6)
                for i in range(4):
                    dve.wait_ge(sem("x_combined"), v * 4 + i + 1)
                    x = xs[:, i % 2, i // 2 * 512:(i // 2 + 1) * 512]
                    nc.vector.tensor_tensor(x, x, bank[(3, 6, 7, 2)[i]][:], ALU.add).then_inc(sem("x_added"), 1)

            with dve.Fori(0, last_visit) as v:
                visit(v, False)
            with dve.Fori(last_visit, last_visit + 1) as v:
                visit(v, True)

            r = roots("n6", TT)
            dve.wait_ge(sem("last_gain_landed"), 16)
            for t in range(TT):
                nc.vector.scalar_tensor_tensor(xs[:, TT + t, :], xs[:, t, :], r[:, t:t + 1], gate_b[:, 1, :], ALU.mult, ALU.mult)\
                  .then_inc(sem("y_done"), 1)

        @block.gpsimd
        def _(pool):
            def root(st, tiles):
                pool.wait_ge(*reached(st, "mean", 1))
                nc.gpsimd.tensor_tensor(stat[:, 8:8 + tiles], stat[:, 4:4 + tiles], minus_half[:, 0:tiles], ALU.pow)\
                  .then_inc(stage_sem["root"], 1)

            pool.wait_ge(sem("ones_ready"), 2)
            root("n0", 4)
            for w in range(2):
                pool.dma_start(gate_b[:, w, :], bass.AP(A["b_mod"].tensor, 2 * D, [[0, P], [1, D]])).then_inc(sem("gate_bias_landed"), 16)
            for j in range(12):
                heads = 8 if j < 8 else 4
                pool.wait_ge(sem("a_qk_mean"), j + 1)
                nc.gpsimd.tensor_tensor(qk_root[:, 0:heads], stat[:, 8:8 + heads], minus_half[:, 0:heads], ALU.pow)\
                  .then_inc(sem("a_qk_root"), 1)
            pool.wait_ge(sem("a_x_done"), 8)
            pool.dma_start(gate_b[:, 0, :], bass.AP(A["b_mod"].tensor, 5 * D, [[0, P], [1, D]])).then_inc(sem("gate_bias_1_landed"), 16)
            pool.dma_start(gate_b[:, 1, :], bass.AP(A["final_norm_g"].tensor, 0, [[0, P], [1, D]]))\
                .then_inc(sem("final_gain_landed"), 16)
            root("n1", 4)
            pool.wait_ge(sem("constants_landed"), 32)
            for h in range(HEADS):
                pool.wait_ge(sem(f"bias_landed_{h % BIAS_RING}"), 64 * (h // BIAS_RING + 1))
                b = near_bias(h).rearrange("p t (r c) -> p t r c", c=GRID_W)
                nc.gpsimd.tensor_tensor(b, b, near.unsqueeze(1).unsqueeze(1).broadcast_to([P, TT, GROWS, GRID_W]), ALU.add)\
                  .then_inc(sem("b_bias_ready"), 1)
            root("f1", TT)
            root("n2", TT)
            root("n3", TT)

            for h in range(HEADS):
                pool.wait_ge(sem(f"bias_landed_{h % BIAS_RING}"), (64 + 32) * (HEADS // BIAS_RING))
                for t, c0, n, b in t5_bias(h):
                    ins = nc.gpsimd.tensor_tensor(b, b, causal[:, c0:c0 + n], ALU.add)
                ins.then_inc(sem("m_bias_ready"), 1)
            root("n4", TT)
            pool.wait_ge(sem("f1_x_done"), 2)
            pool.dma_start(gate_b[:, 0, :], bass.AP(A["ffn_norm_2"].tensor, D, [[0, P], [1, D]])).then_inc(sem("ffn_gain_landed"), 16)
            pool.dma_start(gate_b[:, 1, :], bass.AP(A["final_norm_2"].tensor, 0, [[0, P], [1, D]])).then_inc(sem("last_gain_landed"), 16)
            pool.dma_start(route[:], A["route"]).then_inc(sem("route_landed"), 16)
            pool.dma_start(router_w[:], router.rearrange("(c p) e -> p c e", p=P)).then_inc(sem("route_landed"), 16)
            root("n5", TT)
            for n in (0, 2, 4):
                pool.wait_ge(x_hi_ready, n + 1)
                nc.gpsimd.tensor_tensor(ring6(w_lo, w_lo_x, n, 1)[:, 0, :], ring6(raw, raw_x, n, 1)[:, 0, :],
                                        ring6(w_hi, w_hi_x, n, 1)[:, 0, :].bitcast(F32), ALU.subtract).then_inc(first_rest[0], 1)
            root("n6", TT)

        @block.tensor
        def _(pe):
            def three(out_, a_hi, a_lo, b_hi, b_lo, start, stop):
                nc.tensor.matmul(out_, a_hi, b_hi, start=start, stop=False)
                nc.tensor.matmul(out_, a_hi, b_lo, start=False, stop=False)
                return nc.tensor.matmul(out_, a_lo, b_hi, start=False, stop=stop)

            pe.wait_ge(sem("vectors_landed"), 96)
            pe.wait_ge(sem("constants_landed"), 32)
            nc.tensor.transpose(bank[6][:, 0:NVEC], work[0:NVEC, 0, 0:P], eye[0:NVEC, 0:NVEC]).then_inc(sem("vec_turned"), 1)
            pe.wait_ge(sem("t5_landed"), 32)
            nc.tensor.matmul(bank[7][0:HEADS, 0:T5W], work[0:BUCKETS, 3, 0:HEADS], work[0:BUCKETS, 2, 0:T5W],
                             start=True, stop=True).then_inc(sem("t5_rows"), 1)

            def mod_unit(l, cb, half):
                m = unit_at[f"mod{l}", cb, half]
                pe.wait_ge(lo_ready, m + 1)
                if half == 0 and l == 0 and cb >= 2:
                    pe.wait_ge(sem("mod_ready"), cb - 1)
                if half == 0 and l == 1 and cb:
                    if cb < 5:
                        pe.wait_ge(sem("mod_ready"), 4 + cb)
                    else:
                        pe.wait_ge(sem("mod_row_ready"), 6 + cb)
                hi, lo = unit_view(w_hi, m, 4), unit_view(w_lo, m, 4)
                for c in range(4):
                    k = 4 * half + c
                    nc.tensor.matmul(mod_bank(l, cb)[0:4, :], c_parts[:, k, :], hi[:, c, :], start=(k == 0), stop=False)
                    ins = nc.tensor.matmul(mod_bank(l, cb)[0:4, :], c_parts[:, k, :], lo[:, c, :], start=False, stop=(k == CH - 1))
                ins.then_inc(w_used, 1)

            def turn_mod(l, cb):
                pe.wait_ge(sem("mod_row_ready"), 6 * l + cb + 1)
                for i in range(4):
                    ins = nc.tensor.matmul(mod_bank(l, cb)[:, 2 * i:2 * i + 2], mod_row_of(cb)[:, i * P:(i + 1) * P], spread[:, ::P],
                                           start=True, stop=True)
                ins.then_inc(sem("mod_turned"), 1)

            pe.wait_ge(sem("c_parts_ready"), 1)
            pe.wait_ge(sem("spread_landed"), 16)
            for cb in range(6):
                mod_unit(0, cb, 0)
                if 1 <= cb <= 4:
                    turn_mod(0, cb - 1)
                mod_unit(0, cb, 1)
            pe.wait_ge(sem("t5_copied"), 1)
            pe.wait_ge(sem("mod_row_ready"), 6)

            def norm(st, tiles):
                pe.wait_ge(*reached(st, "diag", tiles))
                for c in range(CH):
                    if c >= 4:
                        pe.wait_ge(*reached(st, "h_lo", c - 3))
                    for t in range(tiles):
                        last = nc.tensor.matmul(bank[4 + c % 4][:, t * P:(t + 1) * P], xs[:, t, c * P:(c + 1) * P], diag[:, t, :],
                                                start=True, stop=True)
                    last.then_inc(stage_sem["transposed"], 1)
                pe.wait_ge(*reached(st, "h_lo", CH // 2))

            def linear(name, blocks, forms, after=None, st=None):
                g = group_at[name]
                for cb in range(blocks):
                    form = forms(cb)
                    for half in range(2):
                        m = unit_at[name, cb, half]
                        pe.wait_ge(lo_ready, m + 1)
                        if st and cb == 0 and half:
                            pe.wait_ge(*reached(st, "h_lo", CH))
                        hi, lo = unit_view(w_hi, m, 4), unit_view(w_lo, m, 4)
                        for i, f in enumerate(form):
                            if half == 0 and g + i >= 4:
                                who, n = emptied_by(g + i - 4)
                                pe.wait_ge(emptied[who], n)
                            b = bank[(g + i) % 4]
                            for c in range(4):
                                k = 4 * half + c
                                first_, last_ = half == 0 and c == 0, half == 1 and c == 3
                                if f[0] == "rows":
                                    cols = slice(f[1] * P, (f[1] + 1) * P)
                                    ins = three(b[:], h_hi[:, k, cols], h_lo[:, k, cols], hi[:, c, :], lo[:, c, :], first_, last_)
                                else:
                                    cols = slice(f[1] * P, (f[1] + 1) * P)
                                    ins = three(b[:, 0:f[2]], hi[:, c, cols], lo[:, c, cols], h_hi[:, k, 0:f[2]], h_lo[:, k, 0:f[2]],
                                                first_, last_)
                            if half:
                                ins.then_inc(product, 1)
                        if not half:
                            ins.then_inc(w_used, 1)
                    g += len(form)
                    if after:
                        after(cb)

            def attention(st):
                plan, lag = plans[st], LAG[st]
                starts, n = group_starts(st), len(plan)
                for i in range(n + lag + 1):
                    if i < n:
                        h, segs, _ = plan[i]
                        par = h % 2 * HD
                        ring = len(S_BANK[st])
                        if i >= ring:
                            if st == "s":
                                pe.wait_ge(sem("s_log_weight"), i - ring + 1)
                            else:
                                pe.wait_ge(*reached(st, "exp", i - ring + 1))
                        b = bank[S_BANK[st][i % len(S_BANK[st])]]
                        for t, q0, k0, nk, c0 in segs:
                            last = nc.tensor.matmul(b[:, c0:c0 + nk], query_operand(st, h, q0),
                                                    key_operand(st, h, k0, nk), start=True, stop=st != "s")
                            if st == "s":
                                last = nc.tensor.matmul(b[:, c0 + nk - P:c0 + nk], eye, negstrict, start=False, stop=True)
                        last.then_inc(stage_sem["scores"], 1)
                    u = i - lag
                    if 0 <= u < n:
                        pe.wait_ge(*reached(st, "prob", u + 1))
                        if u >= 2:
                            pe.wait_ge(*reached(st, "prob_t", u - 1))
                        w = sum(x[3] for x in plan[u][1])
                        source = weight_slot(u) if st == "s" else prob[:, u % 3, :]
                        for k in range(w // P):
                            last = nc.tensor.transpose(bank[T_BANK[u % 2]][:, k * P:(k + 1) * P], source[:, k * P:(k + 1) * P], eye)
                        last.then_inc(stage_sem["prob_turned"], 1)
                    u = i - lag - 1
                    if 0 <= u < n:
                        h, segs, p = plan[u]
                        par = h % 2 * HD
                        if u in starts and p >= 2:
                            pe.wait_ge(*reached(st, "gated", p - 1))
                        pe.wait_ge(*reached(st, "prob_t", u + 1))
                        b = bank[O_BANK[p % 2]]
                        for t, q0, k0, nk, c0 in segs:
                            for k in range(nk // P):
                                last = nc.tensor.matmul(b[par:par + HD, t * P:(t + 1) * P], value_operand(st, h, k0 // P + k),
                                                        prob_t[:, u % 2, c0 + k * P:c0 + (k + 1) * P],
                                                        start=(k == 0), stop=(k == nk // P - 1))
                        last.then_inc(stage_sem["mixed"], 1)
                pe.wait_ge(*reached(st, "out_lo", max(group_ends(st).values()) + 1))

            def spread_gates(w, n0):
                for half in range(2):
                    nc.tensor.matmul(bank[4 + (n0 + half) % 4][:], spread[:, w * P:(w + 1) * P], gate_row[:, half * 512:(half + 1) * 512],
                                     start=True, stop=True).then_inc(sem("gate_spread"), 1)

            rows = lambda n: [("rows", t) for t in range(n)]
            cols = lambda n: [("cols", i, n) for i in range(4)]

            norm("n0", 4)

            def turn_a(cb):
                if cb == 0:
                    spread_gates(0, 0)
                    spread_gates(1, 2)
                    pe.wait_ge(sem("gate_ready"), 4)
                for c in mod_after[cb]:
                    for half in range(2):
                        mod_unit(1, c, half)
                turn_qk(cb)
                if cb < 4:
                    turn_mod(1, cb)

            def turn_qk(cb):
                if not 1 <= cb <= 3:
                    return
                for tt in range(4):
                    j = 4 * (cb - 1) + tt
                    pe.wait_ge(sem("a_qk_done"), j + 1)
                    if j >= 3:
                        pe.wait_ge(sem("a_qk_kept"), j - 2)
                    for k in range(4):
                        last = nc.tensor.transpose(bank[4 + j % 3][:, k * P:(k + 1) * P], qk_slot(j)[:, k * P:(k + 1) * P], eye)
                    last.then_inc(sem("a_qk_turned"), 1)

            linear("a_in", 5, lambda cb: rows(4) if cb < 3 else cols(2 * TOK), turn_a, "n0")
            pe.wait_ge(sem("a_qk_kept"), 12)
            pe.wait_ge(sem("mod_row_ready"), 12)
            pe.wait_ge(emptied["act"], group_at["a_out"])
            attention("a")
            linear("a_out", 2, lambda cb: rows(4))

            norm("n1", 4)
            linear("b_in", 8, lambda cb: cols(TOK) if cb < 2 or cb >= 6 else cols(2 * TOK) if cb < 4 else rows(4),
                   lambda cb: cb == 0 and spread_gates(0, 4), "n1")
            pe.wait_ge(emptied["act"], emptied_by(group_at["b_in"] + 31)[1])
            attention("b")
            linear("b_out", 2, lambda cb: rows(2))

            norm("n2", 2)
            linear("qkv0", 6, lambda cb: cols(TOK) if cb < 4 else rows(2), None, "n2")
            pe.wait_ge(emptied["act"], emptied_by(group_at["qkv0"] + 19)[1])
            attention("s")
            linear("o0", 2, lambda cb: rows(2))
            norm("n3", 2)
            g0 = group_at["ff"]

            def ff_out(j):
                m = ff_at[2, j]
                pe.wait_ge(lo_ready, m + 1)
                pe.wait_ge(sem("ff_hid_lo"), j + 1)
                hi, lo = unit_view(w_hi, m, 2), unit_view(w_lo, m, 2)
                for t in range(TT):
                    for half in range(2):
                        for c in range(2):
                            tok = slice(c * TOK + t * P, c * TOK + (t + 1) * P)
                            n = slice(half * 512, (half + 1) * 512)
                            ins = three(bank[4 + 2 * t + half][:], hid_hi[:, j % 2, tok], hid_lo[:, j % 2, tok], hi[:, c, n], lo[:, c, n],
                                        j == 0 and c == 0, j == HF - 1 and c == 1)
                        if j == HF - 1 and (t, half) != (1, 1):
                            ins.then_inc(sem("ff_out_ready"), 1)
                ins.then_inc(w_used, 1)

            for j in range(HF):
                for kind in (1, 3):
                    m = ff_at[kind, j]
                    g = g0 + 2 * j + (kind == 3)
                    pe.wait_ge(lo_ready, m + 1)
                    who, n = emptied_by(g - 4)
                    pe.wait_ge(emptied[who], n)
                    hi, lo = unit_view(w_hi, m, 8), unit_view(w_lo, m, 8)
                    for i in range(2):
                        for c in range(CH):
                            if g == g0 and c == CH // 2:
                                pe.wait_ge(*reached("n3", "h_lo", CH))
                            f = slice(i * P, (i + 1) * P)
                            ins = three(bank[g % 4][:, i * TOK:(i + 1) * TOK], hi[:, c, f], lo[:, c, f], h_hi[:, c, 0:TOK], h_lo[:, c, 0:TOK],
                                        c == 0, c == CH - 1)
                    ins.then_inc(product, 1)
                if j:
                    ff_out(j - 1)
            ff_out(HF - 1)
            norm("n4", 2)
            linear("qkv1", 6, lambda cb: cols(TOK) if cb < 4 else rows(2), None, "n4")
            pe.wait_ge(emptied["act"], emptied_by(group_at["qkv1"] + 19)[1])
            attention("m")
            linear("o1", 2, lambda cb: rows(2))

            pe.wait_ge(product, len(group_engine))
            pe.wait_ge(*x_done_in("o1"))
            for i in range(6):
                pe.nop().then_inc(x_split_free, 1)
            pe.wait_ge(sem("route_landed"), 32)
            pe.wait_ge(sem("n5_h_ready"), TT)
            for t in range(TT):
                for half in range(2):
                    for c in range(4):
                        k = 4 * half + c
                        ins = nc.tensor.transpose(bank[4 + 2 * t + half][:, c * P:(c + 1) * P], xs[:, TT + t, k * P:(k + 1) * P], eye)
                    ins.then_inc(sem("n5_turned"), 1)
            for t in range(TT):
                pe.wait_ge(sem("n5_turned_kept"), 2 * t + 2)
                for c in range(CH):
                    ins = nc.tensor.matmul(bank[3 * (1 - t)][:, 0:EXP], turned_token(t, c // 4)[:, c % 4 * P:(c % 4 + 1) * P], router_w[:, c, :],
                                           start=(c == 0), stop=(c == CH - 1))
                ins.then_inc(sem("logits"), 1)
            pe.wait_ge(sem("chosen"), 1)
            before, every = route[:, 0:P], ones[:, 0:P]
            nc.tensor.matmul(bank[1][:, 0:EXP], before, facts[:, 2, :], start=True, stop=True).then_inc(sem("slots"), 1)
            nc.tensor.matmul(bank[2][:, 0:EXP], before, facts[:, 3, :], start=True, stop=False)
            nc.tensor.matmul(bank[2][:, 0:EXP], every, facts[:, 2, :], start=False, stop=True).then_inc(sem("slots"), 1)
            nc.tensor.matmul(bank[4][:, 0:EXP], every, facts[:, 2, :], start=True, stop=False)
            nc.tensor.matmul(bank[4][:, 0:EXP], every, facts[:, 3, :], start=False, stop=True).then_inc(sem("slots"), 1)

            def gather(v):
                pe.wait_ge(sem("pick_ready"), v + 1)
                for b in range(2):
                    for c in range(4):
                        for t in range(TT):
                            k = 4 * b + c
                            ins = nc.tensor.matmul(bank[6 + b][:, c * P:(c + 1) * P], xs[:, TT + t, k * P:(k + 1) * P], pick[:, t, :],
                                                   start=(t == 0), stop=(t == TT - 1))
                    ins.then_inc(sem("x_gathered"), 1)

            def expert_unit(v, n, kind, j, half, first=False):
                if first:
                    pe.wait_ge(first_rest[n], 1)
                else:
                    pe.wait_ge(x_raw_free, v * NV + n + 7)
                hi, lo = ring6(w_hi, w_hi_x, n, 4), ring6(w_lo, w_lo_x, n, 4)
                for c in range(4):
                    if kind == 2:
                        a = slice(c * P, (c + 1) * P)
                        ins = three(bank[4 + half][:], act_hi[:, a], act_lo[:, a], hi[:, c, :], lo[:, c, :],
                                    j == 0 and c == 0, j == NJ - 1 and c == 3)
                    else:
                        ins = three(bank[kind // 2][:], xe_hi[:, 4 * half + c, :], xe_lo[:, 4 * half + c, :], hi[:, c, :], lo[:, c, :],
                                    half == 0 and c == 0, half == 1 and c == 3)
                ins.then_inc(x_split_free, 1)

            gather(0)
            pe.wait_ge(sem("xe_lo_ready"), 2)
            for half in range(2):
                expert_unit(0, half, 1, 0, half, True)
            pe.wait_ge(sem("routed"), 1)
            last_visit = pe.value_load(ids[0:1, 12:13], min_val=EXP - 1, max_val=EXP + MAXOVER - 1)

            def visit(v, last):
                def turn(j):
                    pe.wait_ge(sem("act_f_ready"), v * NJ + j + 1)
                    for c in range(4):
                        ins = nc.tensor.transpose(bank[2][:, c * P:(c + 1) * P], act_f[:, c * P:(c + 1) * P], eye)
                    ins.then_inc(sem("x_turned"), 1)

                for n, kind, j, half in visit_steps(last):
                    if kind == 1 and half == 0 and j:
                        pe.wait_ge(sem("act_s_ready"), v * NJ + j)
                    if kind == 3 and half == 0 and j:
                        if j == 1:
                            pe.wait_ge(sem("x_added"), v * 4 + 4)
                        turn(j - 1)
                        if j == 2:
                            pe.wait_ge(sem("pick_g_ready"), v + 1)
                            for t in range(TT):
                                ins = nc.tensor.transpose(bank[3][:, t * P:(t + 1) * P], pick_g[:, t, :], eye)
                            ins.then_inc(sem("pick_turned"), 1)
                    if kind == 2 and half == 0:
                        if j == NJ - 2 and not last:
                            gather(v + 1)
                        if j == NJ - 1 and last:
                            turn(j)
                        pe.wait_ge(sem("act_lo_ready"), v * NJ + j + 1)
                    if kind == 1 and half == 0 and j == 0:
                        turn(NJ - 1)
                        pe.wait_ge(sem("act_s_ready"), v * NJ + NJ)
                        pe.wait_ge(sem("xe_lo_ready"), v * 2 + 4)
                    expert_unit(v, n, kind, j, half)
                pe.wait_ge(sem("pick_gt_ready"), v + 1)
                for i in range(4):
                    t, half = i % 2, i // 2
                    if t == 0:
                        pe.wait_ge(sem("y_ready"), v * 2 + half + 1)
                    nc.tensor.matmul(bank[(3, 6, 7, 2)[i]][:], pick_gt[:, t * P:(t + 1) * P], y_e[:, half * 512:(half + 1) * 512],
                                     start=True, stop=True).then_inc(sem("x_combined"), 1)

            with pe.Fori(0, last_visit) as v:
                visit(v, False)
            with pe.Fori(last_visit, last_visit + 1) as v:
                visit(v, True)


INPUTS = ["x", "c", "ctx", "c_ctx", "norm_g", "w_mod", "b_mod", "a_w_in", "a_q_norm_g", "a_k_norm_g", "a_w_out", "b_w_in",
          "b_rpb", "b_w_out", "final_norm_g", "w_qkv_2", "w_o_2", "mixer_norm_2", "ffn_norm_2", "rel_bias_2", "w1_2", "w3_2",
          "w2_2", "router_2", "e_w1_2", "e_w3_2", "e_w2_2", "final_norm_2"]

def kernel(**inputs):
    import concourse.bacc as bacc
    from concourse.bass_utils import run_bass_kernel_spmd
    nc = bacc.Bacc("TRN2", target_bir_lowering=False, num_devices=1)
    arrays = {name: np.ascontiguousarray(inputs[name]) for name in INPUTS}
    arrays.update(zip(("keep", "once", "onehot", "route", "spread"), shape_constants()))
    A = {k: nc.dram_tensor("in_" + k, a.shape, mybir.dt.from_np(a.dtype), kind="ExternalInput").ap() for k, a in arrays.items()}
    out = nc.dram_tensor("out_0", (1, TOK, D), F32, kind="ExternalOutput").ap()
    build(nc, A, out)
    r = run_bass_kernel_spmd(nc, [{"in_" + k: a for k, a in arrays.items()}], core_ids=[0])
    return r.results[0]["out_0"]
```
